# Optimizing a Trainium2 kernel written in Bass

```python
import jax, jax.numpy as jnp
from jax import lax
import numpy as np

D_MODEL = 2048
BATCH = 1
SEQ = 256
DEPTH = 2

CHUNK = 64
D_MIX = D_MODEL
F32 = jnp.float32

A_HEAD_DIM = 128
A_HEADS = (D_MIX // 2) // A_HEAD_DIM
IDX_HEADS = 16
IDX_DIM = 64
IDX_W_SCALE = (IDX_HEADS * IDX_DIM) ** -0.5
TOPK_MAX = 256
Q_BLOCK = 128
ROPE_THETA = 500000.0
ROPE_FRAC = 4

R_HEADS = 4
R_V_DIM = (D_MIX // 4) // R_HEADS
R_QK_DIM = R_V_DIM // 2
R_THETA = 10000.0

W_HEAD_DIM = 64
W_HEADS = (D_MIX // 4) // W_HEAD_DIM
DECAY_LORA = 96
AAA_LORA = 96
MV_LORA = 64
GATE_LORA = 256
LNX_EPS = 64e-5

D_FF = -(-(8 * D_MODEL) // (3 * 256)) * 256

A_W = A_HEADS * A_HEAD_DIM
B_QK_W = R_HEADS * R_QK_DIM
B_V_W = R_HEADS * R_V_DIM
C_W = W_HEADS * W_HEAD_DIM
SPLIT_AB = [A_W, A_W, A_W, IDX_HEADS * IDX_DIM, IDX_DIM, IDX_HEADS, B_QK_W, B_QK_W, B_V_W, B_V_W]
SPLIT_C = [C_W, C_W, C_W, DECAY_LORA, AAA_LORA, GATE_LORA]
N_AB = sum(SPLIT_AB)
N_C = sum(SPLIT_C)
N_IN = N_AB + N_C

kernel_name = 'hybrid_dsa_retention_rwkv7_chunk_encoder'

def split_cols(t, sizes):
    offs, acc = [], 0
    for s in sizes[:-1]:
        acc += s
        offs.append(acc)
    return jnp.split(t, offs, axis=-1)

def heads(t, n, d):
    return t.reshape(t.shape[0], t.shape[1], n, d)

def rms_norm(x, g, eps=1e-5):
    xf = x.astype(F32)
    y = xf * lax.rsqrt(jnp.mean(xf * xf, axis=-1, keepdims=True) + eps)
    return (y * g.astype(F32)).astype(x.dtype)

def head_norm(y, eps):
    yf = y.astype(F32)
    mu = jnp.mean(yf, axis=-1, keepdims=True)
    var = jnp.mean(jnp.square(yf - mu), axis=-1, keepdims=True)
    return (yf - mu) * lax.rsqrt(var + eps)

def rope(x, pos, rot_dim, theta):
    half = rot_dim // 2
    freqs = jnp.power(F32(theta), -jnp.arange(half, dtype=F32) / half)
    ang = pos.astype(F32)[:, None] * freqs[None, :]
    cos = jnp.cos(ang)[:, None, :]
    sin = jnp.sin(ang)[:, None, :]
    xf = x.astype(F32)
    x1, x2, rest = xf[..., :half], xf[..., half:rot_dim], xf[..., rot_dim:]
    return jnp.concatenate([x1 * cos - x2 * sin, x2 * cos + x1 * sin, rest], axis=-1).astype(x.dtype)

def token_shift(p, mu):
    prev = jnp.pad(p, ((0, 0), (1, 0), (0, 0)))[:, :-1]
    return p + (prev - p) * mu

def sparse_indexer_attention(q, k, v, q_idx, k_idx, w_idx):
    bsz, seq = q.shape[0], q.shape[1]
    top_k = min(TOPK_MAX, seq // 4)
    n_blk = seq // Q_BLOCK
    key_chunk = jnp.arange(seq) // CHUNK
    qpos = jnp.arange(seq).reshape(n_blk, Q_BLOCK)
    scale = A_HEAD_DIM ** -0.5
    gather = jax.vmap(lambda src, ii: src[ii])

    def to_blocks(t):
        return jnp.moveaxis(t.reshape((bsz, n_blk, Q_BLOCK) + t.shape[2:]), 1, 0)

    def one_block(args):
        qb, qib, wb, pb = args
        q_chunk = pb // CHUNK
        rel = jax.nn.relu(jnp.einsum('bqhd,bsd->bqhs', qib, k_idx).astype(F32))
        score = jnp.einsum('bqhs,bqh->bqs', rel, wb.astype(F32))
        adm = key_chunk[None, :] <= q_chunk[:, None]
        score = jnp.where(adm[None], score, -jnp.inf)
        _, idx = lax.top_k(score, top_k)
        valid = (idx // CHUNK) <= q_chunk[None, :, None]
        kg = gather(k, idx)
        vg = gather(v, idx)
        s = jnp.einsum('bqhd,bqkhd->bhqk', qb, kg).astype(F32) * scale
        s = jnp.where(valid[:, None], s, -jnp.inf)
        p = jax.nn.softmax(s, axis=-1).astype(v.dtype)
        return jnp.einsum('bhqk,bqkhd->bqhd', p, vg)

    out = lax.map(one_block, (to_blocks(q), to_blocks(q_idx), to_blocks(w_idx), qpos))
    return jnp.moveaxis(out, 0, 1).reshape(bsz, seq, -1)

def retention(q, k, v):
    bsz, seq, nh, dk = q.shape
    dv = v.shape[-1]
    nc = seq // CHUNK
    log_g = jnp.log1p(-jnp.power(2.0, -5.0 - jnp.arange(nh, dtype=F32)))
    pos = jnp.arange(CHUNK, dtype=F32)
    diff = pos[:, None] - pos[None, :]
    decay = jnp.where(diff >= 0, jnp.exp(jnp.maximum(diff, 0.0)[None] * log_g[:, None, None]), 0.0)
    zeta = jnp.exp((CHUNK - 1.0 - pos)[None, :] * log_g[:, None])
    xi = jnp.exp((pos + 1.0)[None, :] * log_g[:, None])
    g_chunk = jnp.exp(CHUNK * log_g)
    qc = q.astype(F32).reshape(bsz, nc, CHUNK, nh, dk)
    kc = k.astype(F32).reshape(bsz, nc, CHUNK, nh, dk) * dk ** -0.5
    vc = v.astype(F32).reshape(bsz, nc, CHUNK, nh, dv)
    scores = jnp.einsum('bcnhd,bcmhd->bchnm', qc, kc) * decay
    intra = jnp.einsum('bchnm,bcmhe->bcnhe', scores, vc)
    kv = jnp.einsum('bcmhd,bcmhe,hm->bchde', kc, vc, zeta)

    def step(state, kv_c):
        return state * g_chunk[None, :, None, None] + kv_c, state

    _, prev = lax.scan(step, jnp.zeros((bsz, nh, dk, dv), F32), jnp.moveaxis(kv, 1, 0))
    cross = jnp.einsum('bcnhd,cbhde,hn->bcnhe', qc, prev, xi)
    return (intra + cross).reshape(bsz, seq, nh, dv)

def wkv7_scan(r, w, k, v, a, b):
    bsz, _, nh, n = r.shape

    def step(state, inp):
        r_t, w_t, k_t, v_t, a_t, b_t = inp
        sa = jnp.einsum('bhij,bhj->bhi', state, a_t)
        state = state * w_t[:, :, None, :] + sa[..., None] * b_t[:, :, None, :] + v_t[..., None] * k_t[:, :, None, :]
        return state, jnp.einsum('bhij,bhj->bhi', state, r_t)

    xs = tuple(jnp.moveaxis(t, 1, 0) for t in (r, w, k, v, a, b))
    _, y = lax.scan(step, jnp.zeros((bsz, nh, n, n), F32), xs)
    return jnp.moveaxis(y, 0, 1)

def rwkv7_branch(c, mu, w0, w_lb, a0, a_lb, g_lb, k_k, k_a, r_k, lnx_g, lnx_b, v_first, v0, v_lb):
    bsz, seq = c.shape[0], c.shape[1]
    c = token_shift(c, mu)
    has_vres = v0 is not None
    parts = split_cols(c, (SPLIT_C + [MV_LORA]) if has_vres else SPLIT_C)
    r, k, v, wl, al, gl = parts[:6]
    w_log = -jax.nn.softplus(-(w0 + jnp.tanh(wl) @ w_lb)) - 0.5
    decay = jnp.exp(-jnp.exp(w_log.astype(F32)))
    a = jax.nn.sigmoid(a0 + al @ a_lb)
    g = jax.nn.sigmoid(gl) @ g_lb
    if has_vres:
        v = v + (v_first - v) * jax.nn.sigmoid(v0 + parts[6] @ v_lb)
    else:
        v_first = v
    hs = lambda t: t.reshape(bsz, seq, W_HEADS, W_HEAD_DIM).astype(F32)
    kk = hs(k * k_k)
    kk = kk / jnp.maximum(jnp.sqrt(jnp.sum(kk * kk, axis=-1, keepdims=True)), 1e-12)
    k_h = hs(k * (1.0 + (a - 1.0) * k_a))
    r_h, v_h, a_h = hs(r), hs(v), hs(a)
    y = wkv7_scan(r_h, hs(decay), k_h, v_h, -kk, kk * a_h)
    y = head_norm(y, LNX_EPS).reshape(bsz, seq, C_W) * lnx_g + lnx_b
    bonus = jnp.sum(r_h * k_h * r_k, axis=-1, keepdims=True) * v_h
    out = (y + bonus.reshape(bsz, seq, C_W)) * g
    return out.astype(c.dtype), v_first

def setup_inputs(seed: int = 0) -> dict:
    key = jax.random.key(seed)
    ks = iter(jax.random.split(key, 32))
    nrm = lambda shape, scale: jax.random.normal(next(ks), shape, F32) * scale
    uni = lambda shape, lo, hi: jax.random.uniform(next(ks), shape, F32, lo, hi)
    return {
        'x': nrm((BATCH, SEQ, D_MODEL), 1.0),
        'norm_mix_g': 1.0 + nrm((DEPTH, D_MODEL), 0.02),
        'w_in': nrm((DEPTH, D_MODEL, N_IN), D_MODEL ** -0.5),
        'w_in_vres': nrm((DEPTH - 1, D_MODEL, MV_LORA), D_MODEL ** -0.5),
        'rwkv_mu': uni((DEPTH, N_C), 0.0, 1.0),
        'rwkv_mu_vres': uni((DEPTH - 1, MV_LORA), 0.0, 1.0),
        'rwkv_w0': uni((DEPTH, C_W), -6.0, -1.0),
        'rwkv_w_lora_b': nrm((DEPTH, DECAY_LORA, C_W), 0.1 * DECAY_LORA ** -0.5),
        'rwkv_a0': nrm((DEPTH, C_W), 0.1),
        'rwkv_a_lora_b': nrm((DEPTH, AAA_LORA, C_W), AAA_LORA ** -0.5),
        'rwkv_v0': 1.0 + nrm((DEPTH - 1, C_W), 0.1),
        'rwkv_v_lora_b': nrm((DEPTH - 1, MV_LORA, C_W), MV_LORA ** -0.5),
        'rwkv_g_lora_b': nrm((DEPTH, GATE_LORA, C_W), GATE_LORA ** -0.5),
        'rwkv_k_k': 0.85 + nrm((DEPTH, C_W), 0.02),
        'rwkv_k_a': 1.0 + nrm((DEPTH, C_W), 0.02),
        'rwkv_r_k': nrm((DEPTH, W_HEADS, W_HEAD_DIM), 0.1),
        'rwkv_lnx_g': 1.0 + nrm((DEPTH, C_W), 0.02),
        'rwkv_lnx_b': nrm((DEPTH, C_W), 0.02),
        'w_out': nrm((DEPTH, D_MIX, D_MODEL), D_MIX ** -0.5),
        'norm_ffn_g': 1.0 + nrm((DEPTH, D_MODEL), 0.02),
        'w_gate_up': nrm((DEPTH, D_MODEL, 2 * D_FF), D_MODEL ** -0.5),
        'w_down': nrm((DEPTH, D_FF, D_MODEL), D_FF ** -0.5),
        'final_norm_g': 1.0 + nrm((D_MODEL,), 0.02),
    }

def reference(x, norm_mix_g, w_in, w_in_vres, rwkv_mu, rwkv_mu_vres, rwkv_w0, rwkv_w_lora_b,
              rwkv_a0, rwkv_a_lora_b, rwkv_v0, rwkv_v_lora_b, rwkv_g_lora_b, rwkv_k_k, rwkv_k_a,
              rwkv_r_k, rwkv_lnx_g, rwkv_lnx_b, w_out, norm_ffn_g, w_gate_up, w_down, final_norm_g):
    bsz, seq = x.shape[0], x.shape[1]
    positions = jnp.arange(seq)
    v_first = None
    for l in range(DEPTH):
        h = rms_norm(x, norm_mix_g[l])
        w_full = w_in[l] if l == 0 else jnp.concatenate([w_in[l], w_in_vres[l - 1]], axis=1)
        proj = h @ w_full
        a_q, a_k, a_v, a_qi, a_ki, a_wi, b_q, b_k, b_v, b_g = split_cols(proj[..., :N_AB], SPLIT_AB)
        c_cols = proj[..., N_AB:]

        q = rope(heads(a_q, A_HEADS, A_HEAD_DIM), positions, A_HEAD_DIM // ROPE_FRAC, ROPE_THETA)
        k = rope(heads(a_k, A_HEADS, A_HEAD_DIM), positions, A_HEAD_DIM // ROPE_FRAC, ROPE_THETA)
        v = heads(a_v, A_HEADS, A_HEAD_DIM)
        qi = rope(heads(a_qi, IDX_HEADS, IDX_DIM), positions, IDX_DIM // ROPE_FRAC, ROPE_THETA)
        ki = rope(a_ki[:, :, None, :], positions, IDX_DIM // ROPE_FRAC, ROPE_THETA)[:, :, 0]
        out_a = sparse_indexer_attention(q, k, v, qi, ki, a_wi * IDX_W_SCALE)

        rq = rope(heads(b_q, R_HEADS, R_QK_DIM), positions, R_QK_DIM, R_THETA)
        rk = rope(heads(b_k, R_HEADS, R_QK_DIM), positions, R_QK_DIM, R_THETA)
        ret = retention(rq, rk, heads(b_v, R_HEADS, R_V_DIM))
        out_b = (head_norm(ret, 1e-5).reshape(bsz, seq, B_V_W) * jax.nn.silu(b_g.astype(F32))).astype(x.dtype)

        if l == 0:
            mu_l, v0_l, v_lb_l = rwkv_mu[l], None, None
        else:
            mu_l = jnp.concatenate([rwkv_mu[l], rwkv_mu_vres[l - 1]])
            v0_l, v_lb_l = rwkv_v0[l - 1], rwkv_v_lora_b[l - 1]
        out_c, v_first = rwkv7_branch(c_cols, mu_l, rwkv_w0[l], rwkv_w_lora_b[l], rwkv_a0[l],
                                      rwkv_a_lora_b[l], rwkv_g_lora_b[l], rwkv_k_k[l], rwkv_k_a[l],
                                      rwkv_r_k[l], rwkv_lnx_g[l], rwkv_lnx_b[l], v_first, v0_l, v_lb_l)

        x = x + jnp.concatenate([out_a, out_b, out_c], axis=-1) @ w_out[l]

        h = rms_norm(x, norm_ffn_g[l])
        gate, up = jnp.split(h @ w_gate_up[l], 2, axis=-1)
        x = x + (jax.nn.silu(gate) * up) @ w_down[l]
    return rms_norm(x, final_norm_g)


_drawn_inputs = setup_inputs


def setup_inputs(seed=0):
    import zlib

    import numpy as np

    out = dict(_drawn_inputs(seed))
    spreads = {}
    factors = {'rwkv_w_lora_b': 8.0,
     'rwkv_a0': 3.095,
     'rwkv_v0': 200.0,
     'rwkv_k_k': 15.433,
     'rwkv_k_a': 4.127,
     'rwkv_lnx_g': 4.98,
     'rwkv_lnx_b': 5.145,
     'final_norm_g': 22.487,
     'w_in_vres': 8.0,
     'rwkv_mu_vres': 8.0,
     'rwkv_v_lora_b': 8.0,
     'norm_ffn_g': 3.619}
    for name, (base, spread) in spreads.items():
        noise = np.random.default_rng([zlib.crc32(name.encode()), seed]).standard_normal(out[name].shape)
        drawn = base * np.exp(spread * noise) if base else spread * noise
        out[name] = __import__('jax').numpy.asarray(drawn.astype(out[name].dtype))
    for name, factor in factors.items():
        out[name] = (out[name] * factor).astype(out[name].dtype)
    return out
```

```python
from contextlib import ExitStack

import numpy as np
import concourse.bass as bass
from concourse import mybir

F32 = mybir.dt.float32
F32R = mybir.dt.float32r
ACT = mybir.ActivationFunctionType
ALU = mybir.AluOpType
AX = mybir.AxisListType

P = 128
SEQ, D, DEPTH = 256, 2048, 2
NT = SEQ // P
CH = 64
NCH = SEQ // CH
KT = D // P
TW = 512
KB = 4
BLK = KB * TW

A_HEADS, A_DIM = 8, 128
I_HEADS, I_DIM = 16, 64
R_HEADS, R_QK, R_V = 4, 64, 128
W_HEADS, W_DIM = 8, 64
TOPK = 64
A_HALF, I_HALF, R_HALF = A_DIM // 8, I_DIM // 8, R_QK // 2
A_W, I_W, C_W = A_HEADS * A_DIM, I_HEADS * I_DIM, W_HEADS * W_DIM
DECAY_LORA, AAA_LORA, GATE_LORA, MV_LORA = 96, 96, 256, 64
D_FF = 5632
FT = D_FF // TW
FK = D_FF // P
IDX_W_SCALE = float((I_HEADS * I_DIM) ** -0.5)
A_SCALE = float(A_DIM ** -0.5)
EXP_M_HALF = float(np.exp(-0.5))
EPS, LNX_EPS, KK_EPS = 1e-5, 64e-5, 1e-12
BIG = 1e30
INADMISSIBLE, TAKEN = -1e38, -3e38

Q0, K0, V0 = 0, A_W, 2 * A_W
QI0 = 3 * A_W
KI0 = QI0 + I_W
WI0 = KI0 + I_DIM
BQ0 = WI0 + I_HEADS
BV0 = BQ0 + 2 * R_HEADS * R_QK
BG0 = BV0 + R_HEADS * R_V
C0 = BG0 + R_HEADS * R_V
WL0 = C0 + 3 * C_W
AL0 = WL0 + DECAY_LORA
GL0 = AL0 + AAA_LORA

(T_R, T_K, T_V, T_TAIL, T_NARROW, T_QI0, T_QI1, T_Q0, T_Q1, T_K0, T_K1, T_V0, T_V1,
 T_BQK, T_BV, T_BG) = range(16)
N_TILES = 16
NARROW = I_DIM + I_HEADS + MV_LORA
NARROW_KB = 8
TURNED = (T_R, T_K, T_V, T_TAIL, T_NARROW, T_QI0, T_QI1, T_Q0, T_Q1, T_K0, T_K1, T_BQK)
ROTATED = (T_NARROW, T_QI0, T_QI1, T_Q0, T_Q1, T_K0, T_K1, T_BQK)

def first_block(j):
    return KB * j if j <= T_NARROW else KB * (j - 1) + KT // NARROW_KB

IN_BLOCKS = first_block(N_TILES)
OUT_B0 = IN_BLOCKS
FFN_B0 = OUT_B0 + 4 * (KT // KB)
DOWN_B0 = FFN_B0 + 2 * FT * (KT // KB)
DOWN_PER = FK // KB
LAYER_BLOCKS = DOWN_B0 + 4 * DOWN_PER
N_BLOCKS = DEPTH * LAYER_BLOCKS

VEC = {}
for _name, _n in (("mu_r", 4), ("mu_k", 4), ("mu_v", 4), ("mu_wl", 1), ("mu_al", 1), ("mu_gl", 2),
                  ("mu_vr", 1), ("w0", 4), ("a0", 4), ("v0", 4), ("k_k", 4), ("k_a", 4), ("r_k", 4)):
    VEC[_name] = (sum(n for _, n in VEC.values()), _n)
N_VEC = sum(n for _, n in VEC.values())

CONST = {}
for _name, _n in (("ident", P), ("rope", NT * 2 * (A_HALF + I_HALF + R_HALF)), ("headmask", 4 * 8),
                  ("gram_mask", 4 * CH), ("level_mask", 6 * CH), ("ident64", CH), ("scan", 2 * CH)):
    CONST[_name] = (sum(n for _, n in CONST.values()), _n)
N_CONST = sum(n for _, n in CONST.values())
ROPE_AT = {"A": (0, A_HALF), "I": (2 * A_HALF, I_HALF), "R": (2 * (A_HALF + I_HALF), R_HALF)}


class Flag:

    def __init__(self, sem, per):
        self.sem, self.per = sem, per

    def at(self, layer, k=0):
        return layer * self.per + k + 1


def build(nc, x_in, stream, consts, decay_in, headmask_t, vecs, wlb, alb, vlb, glb, lnx, gain_cols, final_gain, out, v_keep):
    base = (nc.sbuf_base + 63) // 64 * 64
    KIB = 1024
    MIX = base + 120 * KIB

    def place(name, shape, offset, dt=F32):
        return nc.alloc_sbuf_tensor_at(name, shape, dt, offset=offset)

    def mix(name, shape, kib, dt=F32):
        return place(name, shape, MIX + int(kib * KIB), dt)

    with ExitStack() as ctx:
        ps = ctx.enter_context(nc.psum_tensor("ps", [P, 8, 512], F32))

        def flag(name, per):
            return Flag(ctx.enter_context(nc.semaphore(name)), per)

        def sem(name):
            return ctx.enter_context(nc.semaphore(name))

        x = place("x", [P, NT, D], base)
        act_hi = place("act_hi", [P, NT, KT, P], base + 16 * KIB, F32R)
        act_lo = place("act_lo", [P, NT, KT, P], base + 32 * KIB, F32R)
        raw = place("raw", [P, 4, BLK], base + 48 * KIB)
        w_hi = place("w_hi", [P, 2, BLK], base + 80 * KIB, F32R)
        w_lo = place("w_lo", [P, 2, BLK], base + 96 * KIB, F32R)
        cst = place("cst", [P, N_CONST], base + 112 * KIB)
        small_at = [base + 112 * KIB + -(-4 * N_CONST // 32) * 32]

        def small(name, shape):
            t = place(name, shape, small_at[0])
            small_at[0] += -(-4 * int(np.prod(shape[1:])) // 32) * 32
            assert small_at[0] <= MIX
            return t

        vec = small("vec", [P, DEPTH, N_VEC])
        gains = small("gains", [P, 2 * DEPTH * KT])
        inv8 = small("inv8", [8, SEQ])
        chunk_decay = small("chunk_decay", [P, 16])
        bonus = small("bonus", [P, 16])
        wi = small("wi", [P, NT, I_HEADS])
        top8 = small("top8", [P, 8])
        gsum = small("gsum", [P, 16])
        gvar = small("gvar", [P, 16])
        nmax = small("nmax", [P, 8])
        rsum = small("rsum", [P, 8])
        sq_parts = small("sq_parts", [P, NT, 4])
        rstd = small("rstd", [P, NT])

        ff_hi = place("ff_hi", [P, NT, FK, P], MIX, F32R)
        ff_lo = place("ff_lo", [P, NT, FK, P], MIX + 44 * KIB, F32R)
        junk = [mix("junk_down", [P, NT, TW], 88), mix("junk_out", [P, NT, TW], 60)]
        gain_row = place("gain_row", [P, D], base + 16 * KIB)
        cat_h = [mix(f"cat_hi{q}", [P, NT, KB, P], k, F32R) for q, k in enumerate((0, 4, 80, 84))]
        cat_l = [mix(f"cat_lo{q}", [P, NT, KB, P], k, F32R) for q, k in enumerate((8, 12, 24, 88))]
        ff_act = mix("ff_act", [P, NT, TW], 88)
        rT = mix("rT", [P, 4, SEQ], 0)
        kT_c = mix("kT_c", [P, 4, SEQ], 4)
        vT_c = mix("vT_c", [P, 4, SEQ], 8)
        tailT = mix("tailT", [P, 4, SEQ], 12)
        vrT = mix("vrT", [MV_LORA, SEQ], 16)
        shift = mix("shift", [P, 4, SEQ], 17)
        g_tok = mix("g_tok", [P, NT, C_W], 17)
        wlb_sb = mix("wlb_sb", [DECAY_LORA, C_W], 21)
        alb_sb = mix("alb_sb", [AAA_LORA, C_W], 23)
        v_tok_c = mix("v_tok_c", [P, NT, C_W], 21)
        vlb_sb = mix("vlb_sb", [MV_LORA, C_W], 25)
        glb_sb = mix("glb_sb", [P, 2, C_W], 27)
        lnx_sb = mix("lnx_sb", [P, 2, C_W], 31)
        hmt_sb = mix("hmt_sb", [8, C_W], 35)
        Pd = mix("Pd", [P, 4, SEQ], 37)
        w_c = mix("w_c", [P, 4, SEQ], 41)
        a_c = mix("a_c", [P, 4, SEQ], 45)
        kk = mix("kk", [P, 4, SEQ], 49)
        kh = mix("kh", [P, 4, SEQ], 53)
        AR = mix("AR", [P, 16, 2, CH], 57)
        d0 = mix("d0", [P, 4 * SEQ], 57)
        d1 = mix("d1", [P, 4 * SEQ], 61)
        BT = mix("BT", [P, 4, SEQ], 65)
        KTl = mix("KTl", [P, 4, SEQ], 69)
        b_tok = mix("b_tok", [P, NT, C_W], 73)
        k_tok = mix("k_tok", [P, NT, C_W], 77)
        G = mix("G", [P, NT, 8, 4, CH], 0)
        Tm = mix("Tm", [P, NT, 8, CH], 41)
        Tt = mix("Tt", [P, NT, 8, CH], 45)
        Xm = mix("Xm", [P, NT, 8, CH], 49)
        Mk = mix("Mk", [P, NT, 8, CH], 53)
        y_c = mix("y_c", [P, NT, C_W], 37)
        S = mix("S", [P, 4, CH], 65)
        S_tmp = mix("S_tmp", [P, 4, CH], 66)
        S_bd = mix("S_bd", [P, 4, 2, CH], 67)
        W_sb = mix("W_sb", [P, C_W], 69)
        av = mix("av", [P, NT, C_W], 49)
        U_sb = mix("U_sb", [P, C_W], 71)
        yc_c = mix("yc_c", [P, NT, C_W], 41)
        sq_c = mix("sq_c", [P, NT, C_W], 49)
        tok_c = [mix("tok_c0", [P, NT, TW], 73), mix("tok_c1", [P, NT, TW], 77)]
        tok_a = [mix("tok_a0", [P, NT, TW], 0), mix("tok_a1", [P, NT, TW], 4)]
        rope_tmp = mix("rope_tmp", [P, 4, 512], 8)
        qiT = mix("qiT", [P, 8, SEQ], 16)
        kiT = mix("kiT", [P, SEQ], 92)
        ki2 = mix("ki2", [P, NT, 2, I_DIM], 83)
        qT = mix("qT", [P, 8, SEQ], 28)
        kT = mix("kT", [P, 8, SEQ], 36)
        v_tok = mix("v_tok", [P, NT, A_W], 44)
        Sx = [mix("Sx0", [P, 8, P], 60), mix("Sx1", [P, 8, SEQ], 52)]
        PT = [mix("PT0", [P, 8, 1, P], 64), mix("PT1", [P, 8, 2, P], 60)]
        work = mix("work", [P, NT, SEQ], 68)
        relu = mix("relu", [P, 2, 2, 2, SEQ], 52)
        keep = mix("keep", [P, NT, SEQ], 74)
        bT = mix("bT", [P, 4, SEQ], 76)
        bv = mix("bv", [P, NT, TW], 16)
        bg = mix("bg", [P, NT, TW], 20)
        decay = mix("decay", [P, 4, 384], 68)
        SB = mix("SB", [P, 4, 384], 52)
        y_b = mix("y_b", [P, NT, TW], 60)
        yc_b = mix("yc_b", [P, NT, TW], 64)
        sq_b = mix("sq_b", [P, NT, TW], 28)
        tok_n = mix("tok_n", [P, NT, NARROW], 81)

        def const(name):
            at, n = CONST[name]
            return cst[:, at:at + n]

        ident = const("ident")
        headmask = const("headmask").rearrange("p (b h) -> p b h", b=4)
        gram_mask = const("gram_mask")
        level_mask = const("level_mask").rearrange("p (l c) -> p l c", l=6)
        ident64 = const("ident64")
        not_start = const("scan")[:, 0:CH]
        at_start = const("scan")[:, CH:2 * CH]
        rope_tab = const("rope").rearrange("p (t c) -> p t c", t=NT)

        def vcol(layer, name, k=0):
            at = VEC[name][0] + k
            return vec[:, layer, at:at + 1]

        def gain_col(m, k):
            return gains[:, m * KT + k:m * KT + k + 1]

        def vbc(layer, name):
            at = VEC[name][0]
            return vec[:, layer, at:at + 4].unsqueeze(2).to_broadcast([P, 4, SEQ])

        def over_mid(ap, n):
            return ap.unsqueeze(1).to_broadcast([ap.shape[0], n, ap.shape[1]])

        def last(ap, n):
            return ap.unsqueeze(2).to_broadcast([ap.shape[0], ap.shape[1], n])

        def flat(ap):
            names = "abcd"[:len(ap.shape) - 1]
            return ap.rearrange(f"p {' '.join(names)} -> p ({' '.join(names)})")

        def bank(b, w=512):
            return ps[:, b, 0:w]

        def banks(b, n):
            return ps[:, b:b + n, :]

        x_loaded = [sem(f"x_loaded{q}") for q in range(4)]
        consts_loaded, vecs_loaded = sem("consts_loaded"), sem("vecs_loaded")
        raw_loaded = [sem(f"raw_loaded{s}") for s in range(4)]
        hi_ready, lo_ready, mm_done = sem("hi_ready"), sem("lo_ready"), sem("mm_done")
        act_chain, dve_chain = sem("act_chain"), sem("dve_chain")

        gain_loaded = sem("gain_loaded")
        sq_summed, var_ready = sem("sq_summed"), sem("var_ready")
        std_ready, rstd_ready = sem("std_ready"), sem("rstd_ready")
        x_turned = sem("x_turned")
        act_hi_ready, act_lo_ready = sem("act_hi_ready"), sem("act_lo_ready")

        tile_tok = flag("tile_tok", N_TILES)
        tile_rot = flag("tile_rot", len(ROTATED))
        tile_turned = flag("tile_turned", len(TURNED))
        tile_ch = flag("tile_ch", len(TURNED))

        c_params = sem("c_params")
        shifted = flag("shifted", 5)
        lora_in = flag("lora_in", 1)
        zw_ps, za_ps, zv_ps, g_ps = flag("zw_ps", 1), flag("za_ps", 1), flag("zv_ps", 1), flag("g_ps", 1)
        a_ready, w_ready, sv_ready, g_ready = (flag("a_ready", 1), flag("w_ready", 1),
                                               flag("sv_ready", 1), flag("g_ready", 1))
        v_kept, v_first_loaded, v_mixed = flag("v_kept", 16), flag("v_first_loaded", 1), flag("v_mixed", 1)
        sqk_ready, ss_ps, nrm_ready, inv_ready, invb_ps = (flag("sqk_ready", 1), flag("ss_ps", 1),
                                                           flag("nrm_ready", 1), flag("inv_ready", 1),
                                                           flag("invb_ps", 1))
        ark_ready, rkk_ready = flag("ark_ready", 1), flag("rkk_ready", 1)
        turned_c, tok_ready, bonus_ps, bonus_ready = (flag("turned_c", 3), flag("tok_ready", 3),
                                                      flag("bonus_ps", 1), flag("bonus_ready", 1))
        gram_ps, gram_ready = flag("gram_ps", 4), flag("gram_ready", 4)
        mk_ready, x_ps, x_ready = flag("mk_ready", 12), flag("x_ps", 12), flag("x_ready", 10)
        t_ps, t_ready = flag("t_ps", 10), flag("t_ready", 12)
        s_zeroed = flag("s_zeroed", 1)
        pre_ps, pre_ready = flag("pre_ps", 1), flag("pre_ready", 1)
        w_ps, w_sbr, u_ps, u_sbr = flag("w_ps", 3), flag("w_sbr", 3), flag("u_ps", 4), flag("u_sbr", 4)
        y_ps, y_sbr, s_ps, s_sbr = flag("y_ps", 4), flag("y_sbr", 4), flag("s_ps", 3), flag("s_sbr", 3)
        gvar_ready, gstd_ready = flag("gvar_ready", 2), flag("gstd_ready", 2)
        oc_ready, oc_turned = flag("oc_ready", 1), flag("oc_turned", 1)

        score_ps, relu_ready, relu_used = flag("score_ps", 8), flag("relu_ready", 8), flag("relu_used", 8)
        topk_done = flag("topk_done", 1)
        att_ps, masked, exp_ready, p_ready = (flag("att_ps", 2), flag("masked", 2), flag("exp_ready", 2),
                                              flag("p_ready", 2))
        p_turned, pT_ready, pv_ps = flag("p_turned", 2), flag("pT_ready", 2), flag("pv_ps", 2)
        decay_loaded = sem("decay_loaded")
        bs_ps, sb_ready, yb_ps, yb_ready = flag("bs_ps", 1), flag("sb_ready", 1), flag("yb_ps", 1), flag("yb_ready", 1)
        ob_ready, ob_turned = flag("ob_ready", 1), flag("ob_turned", 1)
        cat_hi, cat_lo = flag("cat_hi", 4), flag("cat_lo", 4)
        resid_out, resid_down = flag("resid_out", 4), flag("resid_down", 4)
        silu_ready, ffa_ready, ffa_turned = flag("silu_ready", FT), flag("ffa_ready", FT), flag("ffa_turned", FT)
        ff_hi_ready, ff_lo_ready = flag("ff_hi_ready", FT), flag("ff_lo_ready", FT)
        out_ready, stored = sem("out_ready"), sem("stored")

        block = ctx.enter_context(nc.Block())

        @block.sync
        def _(sp):
            for q in range(4):
                cols = slice(q * TW, (q + 1) * TW)
                sp.dma_start(x[:, :, cols], x_in[:, cols].rearrange("(t p) n -> p t n", p=P))\
                  .then_inc(x_loaded[q], 16)
            for s in range(4):
                sp.dma_start(raw[:, s, :], stream[s * P:(s + 1) * P, :]).then_inc(raw_loaded[s], 16)
            with sp.Fori(1, N_BLOCKS // 4) as i:
                for s in range(4):
                    sp.wait_ge(lo_ready, i * 4 + (s - 3))
                    sp.dma_start(raw[:, s, :], stream[bass.ds(i * (4 * P) + s * P, P), :])\
                      .then_inc(raw_loaded[s], 16)
            for k in range(2 * NT):
                t, cols = k // 2, slice((k % 2) * (D // 2), (k % 2 + 1) * (D // 2))
                sp.wait_ge(out_ready, k + 1)
                sp.dma_start(out[t * P:(t + 1) * P, cols], x[:, t, cols]).then_inc(stored, 16)
            sp.wait_ge(stored, 32 * NT)

        @block.gpsimd
        def _(pool):
            pool.dma_start(cst[:, :], consts).then_inc(consts_loaded, 16)
            pool.dma_start(gains[:, :], gain_cols).then_inc(consts_loaded, 16)
            pool.dma_start(flat(vec[:, :, :]), vecs).then_inc(vecs_loaded, 16)
            for l in range(DEPTH):
                if l > 0:
                    pool.wait_ge(mm_done, LAYER_BLOCKS * l)
                pool.dma_start(wlb_sb[:, :], wlb[l]).then_inc(c_params, 16)
                pool.dma_start(alb_sb[:, :], alb[l]).then_inc(c_params, 16)
                pool.dma_start(vlb_sb[:, :], vlb).then_inc(c_params, 16)
                pool.dma_start(glb_sb[:, :, :], glb[l].rearrange("(k p) n -> p k n", p=P)).then_inc(c_params, 16)
                pool.dma_start(flat(lnx_sb[:, :, :]), lnx[l:l + 1, :].partition_broadcast(P)
                               .rearrange("p a d -> p (a d)")).then_inc(c_params, 16)
                pool.dma_start(hmt_sb[:, :], headmask_t).then_inc(c_params, 16)
                if l == 0:
                    pool.wait_ge(shifted.sem, shifted.at(l, T_V))
                    pool.dma_start(v_keep, flat(vT_c[:, :, :])).then_inc(v_kept.sem, 16)
                else:
                    pool.wait_ge(v_kept.sem, 16)
                    pool.dma_start(flat(kk[:, :, :]), v_keep).then_inc(v_first_loaded.sem, 16)
                pool.wait_ge(topk_done.sem, topk_done.at(l))
                pool.dma_start(flat(decay[:, :, :]), decay_in).then_inc(decay_loaded, 16)
            pool.wait_ge(mm_done, LAYER_BLOCKS * (DEPTH - 1) + DOWN_B0)
            pool.dma_start(gain_row[:, :], final_gain.partition_broadcast(P).rearrange("p a d -> p (a d)"))\
                .then_inc(gain_loaded, 16)

        @block.scalar
        def _(act):
            links = [0]

            def link(ins):
                links[0] += 1
                ins.then_inc(act_chain, 1)
                act.wait_ge(act_chain, links[0])

            def copy(o, i):
                return act.activation(o, i, ACT.Copy)

            def hi_block(n, w=BLK):
                act.wait_ge(raw_loaded[n % 4], (n // 4 + 1) * 16)
                if n >= 2:
                    act.wait_ge(mm_done, n - 1)
                copy(w_hi[:, n % 2, 0:w], raw[:, n % 4, 0:w]).then_inc(hi_ready, 1)

            def x_done(m, q):
                if m == 0:
                    act.wait_ge(x_loaded[q], 16)
                else:
                    r = resid_down if m % 2 == 0 else resid_out
                    act.wait_ge(r.sem, r.at((m - 1) // 2, q))

            def square(m, q):
                x_done(m, q)
                for t in range(NT):
                    act.activation(junk[m % 2][:, t, :], x[:, t, q * TW:(q + 1) * TW], ACT.Square,
                                   accum_out=sq_parts[:, t, q:q + 1]).then_inc(sq_summed, 1)
                act.wait_ge(sq_summed, NT * (4 * m + q + 1))

            def norm_hi(m, q):
                act.wait_ge(x_turned, 4 * m + q + 1)
                if m > 0:
                    act.wait_ge(mm_done, (m - 1) // 2 * LAYER_BLOCKS + (DOWN_B0 if m % 2 == 0 else OUT_B0))
                for c in range(KB):
                    e = act.activation(act_hi[:, :, KB * q + c, :],
                                       banks(4 + 2 * (q % 2), 2)[:, :, c * P:(c + 1) * P], ACT.Copy,
                                       scale=gain_col(m, KB * q + c))
                e.then_inc(act_hi_ready, 1)

            def std(m):
                act.wait_ge(var_ready, m + 1)
                act.activation(rstd[:, :], rstd[:, :], ACT.Sqrt).then_inc(std_ready, 1)

            def start(m, n):
                hi_block(n)
                hi_block(n + 1)
                square(m, 3)
                hi_block(n + 2)
                norm_hi(m, 3)
                std(m)
                hi_block(n + 3)

            def scaled(dst, b0, w=TW, func=ACT.Copy):
                for t in range(NT):
                    e = act.activation(dst[:, t, :], bank(b0 + t, w), func, scale=rstd[:, t:t + 1])
                return e

            act.wait_ge(consts_loaded, 32)
            norm_hi(0, 0)
            hi_block(0)
            norm_hi(0, 1)
            hi_block(1)
            norm_hi(0, 2)
            square(0, 0)
            square(0, 1)
            hi_block(2)
            norm_hi(0, 3)
            square(0, 2)
            square(0, 3)
            std(0)
            hi_block(3)
            for l in range(DEPTH):
                nb = l * LAYER_BLOCKS

                def tile_hi(j):
                    for b in range(first_block(j), first_block(j + 1)):
                        hi_block(nb + b, NARROW_KB * NARROW if j == T_NARROW else BLK)

                def acc(j):
                    act.wait_ge(mm_done, nb + first_block(j + 1))
                    return 2 * (j % 2)

                def to_tok(j, dst, before=None):
                    if before is not None:
                        act.wait_ge(tile_turned.sem, tile_turned.at(l, TURNED.index(before)))
                    scaled(dst, acc(j)).then_inc(tile_tok.sem, 1)

                if l > 0:
                    start(2 * l, nb)
                hi_block(nb + 4)
                hi_block(nb + 5)
                act.wait_ge(rstd_ready, 2 * l + 1)
                to_tok(T_R, tok_c[0][:, :, :])
                hi_block(nb + 6)
                hi_block(nb + 7)
                hi_block(nb + 8)
                hi_block(nb + 9)
                to_tok(T_K, tok_c[1][:, :, :])
                hi_block(nb + 10)
                hi_block(nb + 11)
                hi_block(nb + 12)
                hi_block(nb + 13)
                to_tok(T_V, tok_c[0][:, :, :], T_R)
                hi_block(nb + 14)
                hi_block(nb + 15)
                tile_hi(T_NARROW)
                to_tok(T_TAIL, tok_c[1][:, :, :], T_K)
                act.wait_ge(mm_done, nb + first_block(T_NARROW + 1))
                scaled(tok_n[:, :, :], 0, NARROW).then_inc(tile_tok.sem, 1)

                act.wait_ge(shifted.sem, shifted.at(l, 3))
                act.activation(tailT[:, 0, :], tailT[:, 0, :], ACT.Tanh)
                act.activation(tailT[:, 2:4, :], tailT[:, 2:4, :], ACT.Sigmoid).then_inc(lora_in.sem, 1)
                if l == 0:
                    act.wait_ge(vecs_loaded, 16)
                act.wait_ge(za_ps.sem, za_ps.at(l))
                for b in range(4):
                    last_a = act.activation(a_c[:, b, :], flat(banks(6, 2))[:, b * SEQ:(b + 1) * SEQ], ACT.Sigmoid,
                                            bias=vcol(l, "a0", b))
                last_a.then_inc(a_ready.sem, 1)
                act.wait_ge(zw_ps.sem, zw_ps.at(l))
                for b in range(4):
                    last_w = act.activation(w_c[:, b, :], flat(banks(4, 2))[:, b * SEQ:(b + 1) * SEQ], ACT.Sigmoid,
                                            bias=vcol(l, "w0", b))
                link(last_w)
                act.activation(w_c[:, :, :], w_c[:, :, :], ACT.Exp, scale=-EXP_M_HALF).then_inc(w_ready.sem, 1)
                if l > 0:
                    act.wait_ge(zv_ps.sem, l)
                    for b in range(4):
                        last_v = act.activation(kh[:, b, :], flat(banks(4, 2))[:, b * SEQ:(b + 1) * SEQ],
                                                ACT.Sigmoid, bias=vcol(l, "v0", b))
                    last_v.then_inc(sv_ready.sem, 1)
                act.wait_ge(g_ps.sem, g_ps.at(l))
                act.wait_ge(shifted.sem, shifted.at(l, 4))
                copy(g_tok[:, :, :], banks(6, 2)).then_inc(g_ready.sem, 1)
                act.wait_ge(ss_ps.sem, ss_ps.at(l))
                act.activation(inv8[:, :], ps[0:8, 4, 0:SEQ], ACT.Sqrt).then_inc(nrm_ready.sem, 1)
                for n, (dst, b) in enumerate(((b_tok, 4), (k_tok, 6), (v_tok_c, 4))):
                    act.wait_ge(turned_c.sem, turned_c.at(l, n))
                    copy(dst[:, :, :], banks(b, 2)).then_inc(tok_ready.sem, 1)
                act.wait_ge(bonus_ps.sem, bonus_ps.at(l))
                copy(bonus[:, :], bank(6, 16)).then_inc(bonus_ready.sem, 1)
                for lev in range(1, 6):
                    for t in range(NT):
                        act.wait_ge(x_ps.sem, x_ps.at(l, 2 * lev + t))
                        copy(flat(Xm[:, t, :, :]), bank(4 + 2 * t)).then_inc(x_ready.sem, 1)
                act.wait_ge(pre_ps.sem, pre_ps.at(l))
                copy(av[:, :, :], banks(4, 2))
                copy(y_c[:, :, :], banks(6, 2)).then_inc(pre_ready.sem, 1)
                for c in range(NCH):
                    r = slice((c % 2) * CH, (c % 2) * CH + CH)
                    act.wait_ge(u_ps.sem, u_ps.at(l, c))
                    copy(U_sb[r, :], ps[r, 5, :]).then_inc(u_sbr.sem, 1)

                def group_std(k, n):
                    act.wait_ge(gvar_ready.sem, gvar_ready.at(l, k))
                    act.activation(gvar[:, 0:n], gvar[:, 0:n], ACT.Sqrt).then_inc(gstd_ready.sem, 1)

                group_std(0, 16)
                act.wait_ge(oc_turned.sem, oc_turned.at(l))
                copy(flat(cat_h[3][:, :, :, :]), flat(banks(4, 2))).then_inc(cat_hi.sem, 1)

                def scores(k0, k1):
                    for k in range(k0, k1):
                        ns = P * (k // 4 + 1)
                        act.wait_ge(score_ps.sem, score_ps.at(l, k))
                        if k >= 2:
                            act.wait_ge(relu_used.sem, relu_used.at(l, k - 2))
                        act.activation(relu[:, k % 2, :, :, 0:ns],
                                       banks(4 + 2 * (k % 2), 2).rearrange("p o (a s) -> p o a s", a=2)[:, :, :, 0:ns],
                                       ACT.Relu).then_inc(relu_ready.sem, 1)

                dst = {T_QI0: tok_a[1], T_QI1: tok_a[0], T_Q0: tok_a[1], T_Q1: tok_a[0], T_K0: tok_a[1],
                       T_K1: tok_a[0], T_BQK: tok_a[1]}
                before = {T_Q0: T_QI0, T_Q1: T_QI1, T_K0: T_Q0, T_K1: T_Q1, T_BQK: T_K0}
                tile_hi(T_QI0)
                for j in range(T_QI0, N_TILES):
                    if j + 1 < N_TILES:
                        for b in range(first_block(j + 1), first_block(j + 1) + 2):
                            hi_block(nb + b)
                    if j in dst:
                        to_tok(j, dst[j][:, :, :], before.get(j))
                    elif j in (T_V0, T_V1):
                        to_tok(j, v_tok[:, :, (j - T_V0) * TW:(j - T_V0 + 1) * TW])
                    elif j == T_BV:
                        act.wait_ge(score_ps.sem, score_ps.at(l, 7))
                        to_tok(j, bv[:, :, :])
                    else:
                        scaled(bg[:, :, :], acc(j), func=ACT.Silu).then_inc(tile_tok.sem, 1)
                    if j + 1 < N_TILES:
                        for b in range(first_block(j + 1) + 2, first_block(j + 2)):
                            hi_block(nb + b)
                    if j == T_Q0:
                        scores(0, 4)
                    if j == T_Q1:
                        scores(4, 8)

                for t in range(NT):
                    act.wait_ge(masked.sem, masked.at(l, t))
                    for h in range(A_HEADS):
                        e = act.activation(Sx[t][:, h, :], Sx[t][:, h, :], ACT.Exp, bias=nmax[:, h:h + 1],
                                           accum_out=rsum[:, h:h + 1])
                    e.then_inc(exp_ready.sem, 1)
                    act.wait_ge(p_turned.sem, p_turned.at(l, t))
                    if t == 0:
                        copy(flat(PT[0][:, :, :, :]), flat(banks(2, 2))).then_inc(pT_ready.sem, 1)
                    else:
                        copy(flat(PT[1][:, 0:4, :, :]), flat(banks(4, 2)))
                        copy(flat(PT[1][:, 4:8, :, :]), flat(banks(6, 2))).then_inc(pT_ready.sem, 1)
                    act.wait_ge(pv_ps.sem, pv_ps.at(l, t))
                    for q in range(2):
                        e = copy(flat(cat_h[q][:, t, :, :]), bank(2 * t + q))
                    e.then_inc(cat_hi.sem, 1)
                act.wait_ge(yb_ps.sem, yb_ps.at(l))
                copy(y_b[:, :, :], banks(0, 2)).then_inc(yb_ready.sem, 1)
                group_std(1, 8)
                act.wait_ge(ob_turned.sem, ob_turned.at(l))
                copy(flat(cat_h[2][:, :, :, :]), flat(banks(4, 2))).then_inc(cat_hi.sem, 1)

                for cb in range(4):
                    for b in range(KB):
                        hi_block(nb + OUT_B0 + KB * cb + b)
                        if cb > 0 and b == 2:
                            square(2 * l + 1, cb - 1)
                    if cb > 0:
                        norm_hi(2 * l + 1, cb - 1)

                def ffn(i, first):
                    n0 = nb + FFN_B0 + i * 8
                    g = i * 1 + (l * FT)

                    def hi_at(b):
                        s4 = (nb + FFN_B0 + b) % 4
                        act.wait_ge(raw_loaded[s4], i * 32 + ((nb + FFN_B0 + b) // 4 + 1) * 16)
                        act.wait_ge(mm_done, n0 + (b - 1))
                        copy(w_hi[:, b % 2, :], raw[:, s4, :]).then_inc(hi_ready, 1)

                    if first:
                        start(2 * l + 1, n0)
                        act.wait_ge(rstd_ready, 2 * l + 2)
                    else:
                        for b in range(4):
                            hi_at(b)
                        act.wait_ge(ffa_turned.sem, g)
                        turned_hi(i - 1, g)
                    hi_at(4)
                    hi_at(5)
                    act.wait_ge(mm_done, n0 + 4)
                    scaled(ff_act, 0, func=ACT.Silu).then_inc(silu_ready.sem, 1)
                    hi_at(6)
                    hi_at(7)

                def turned_hi(i, g):
                    for t in range(NT):
                        e = copy(flat(ff_hi[:, t, :, :])[:, bass.ds(i * 512, 512)], bank(4 + t))
                    e.then_inc(ff_hi_ready.sem, 1)

                ffn(0, True)
                with act.Fori(1, FT) as i:
                    ffn(i, False)
                act.wait_ge(ffa_turned.sem, FT * (l + 1))
                turned_hi(FT - 1, FT * (l + 1))
                for cb in range(4):
                    for b in range(DOWN_PER):
                        hi_block(nb + DOWN_B0 + DOWN_PER * cb + b)
                        if cb > 0 and b == 3:
                            square(2 * l + 2, cb - 1)
                        if cb > 0 and b == 4 and l < DEPTH - 1:
                            norm_hi(2 * l + 2, cb - 1)
            square(2 * DEPTH, 3)
            std(2 * DEPTH)

        @block.vector
        def _(dve):
            links = [0]

            def link(ins):
                links[0] += 1
                ins.then_inc(dve_chain, 1)
                dve.wait_ge(dve_chain, links[0])

            tt, ts, stt = dve.tensor_tensor, dve.tensor_scalar, dve.scalar_tensor_tensor

            def lo_part(o, i, h):
                return tt(o, i, h.bitcast(F32), ALU.subtract)

            def lo_block(n, w=BLK):
                dve.wait_ge(hi_ready, n + 1)
                lo_part(w_lo[:, n % 2, 0:w], raw[:, n % 4, 0:w], w_hi[:, n % 2, 0:w]).then_inc(lo_ready, 1)

            def norm_lo(m, q):
                dve.wait_ge(act_hi_ready, 4 * m + q + 1)
                for c in range(KB):
                    k = KB * q + c
                    e = stt(act_lo[:, :, k, :], banks(4 + 2 * (q % 2), 2)[:, :, c * P:(c + 1) * P], gain_col(m, k),
                            act_hi[:, :, k, :].bitcast(F32), ALU.mult, ALU.subtract)
                e.then_inc(act_lo_ready, 1)

            def var(m):
                dve.wait_ge(sq_summed, 4 * NT * (m + 1))
                link(dve.tensor_reduce(rstd[:, :], sq_parts[:, :, :], AX.X, ALU.add))
                ts(rstd[:, :], rstd[:, :], 1.0 / D, EPS, ALU.mult, ALU.add).then_inc(var_ready, 1)

            def invert_std(m):
                dve.wait_ge(std_ready, m + 1)
                dve.reciprocal(rstd[:, :], rstd[:, :]).then_inc(rstd_ready, 1)

            def residual(r, l, cb):
                per = KB if r is resid_out else DOWN_PER
                dve.wait_ge(mm_done, l * LAYER_BLOCKS + (OUT_B0 if r is resid_out else DOWN_B0) + per * (cb + 1))
                v = x[:, :, cb * TW:(cb + 1) * TW]
                tt(v, v, banks(2 * (cb % 2), 2), ALU.add).then_inc(r.sem, 1)

            def start(m, n):
                lo_block(n)
                residual(resid_down if m % 2 == 0 else resid_out, (m - 1) // 2, 3)
                lo_block(n + 1)
                var(m)
                lo_block(n + 2)
                norm_lo(m, 3)
                invert_std(m)
                lo_block(n + 3)

            dve.wait_ge(consts_loaded, 32)
            for q in range(4):
                norm_lo(0, q)
                if q < 3:
                    lo_block(q)
            var(0)
            invert_std(0)
            lo_block(3)

            def rope(X, kind, heads):
                at, half = ROPE_AT[kind]
                cos = rope_tab[:, :, at:at + half].unsqueeze(2).to_broadcast([P, NT, heads, half])
                sin = rope_tab[:, :, at + half:at + 2 * half].unsqueeze(2).to_broadcast([P, NT, heads, half])
                x1, x2 = X[:, :, :, 0:half], X[:, :, :, half:2 * half]
                tmp = [rope_tmp[:, k, 0:NT * heads * half].rearrange("p (t h f) -> p t h f", t=NT, h=heads)
                       for k in range(4)]
                tt(tmp[0], x1, cos, ALU.mult)
                tt(tmp[1], x2, sin, ALU.mult)
                tt(tmp[2], x2, cos, ALU.mult)
                link(tt(tmp[3], x1, sin, ALU.mult))
                tt(x1, tmp[0], tmp[1], ALU.subtract)
                return tt(x2, tmp[2], tmp[3], ALU.add)

            def head_norm(l, k, y, yc, sq, groups, eps):
                w = NT * 512 // groups
                yg, ycg, sqg = (flat(z).rearrange("p (g w) -> p g w", g=groups) for z in (y, yc, sq))
                link(dve.tensor_reduce(gsum[:, 0:groups], yg, AX.X, ALU.add))
                link(ts(gsum[:, 0:groups], gsum[:, 0:groups], 1.0 / w, None, ALU.mult))
                link(tt(ycg, yg, last(gsum[:, 0:groups], w), ALU.subtract))
                link(tt(sqg, ycg, ycg, ALU.mult))
                link(dve.tensor_reduce(gvar[:, 0:groups], sqg, AX.X, ALU.add))
                ts(gvar[:, 0:groups], gvar[:, 0:groups], 1.0 / w, eps, ALU.mult, ALU.add).then_inc(gvar_ready.sem, 1)
                dve.wait_ge(gstd_ready.sem, gstd_ready.at(l, k))
                link(dve.reciprocal(gvar[:, 0:groups], gvar[:, 0:groups]))
                link(tt(ycg, ycg, last(gvar[:, 0:groups], w), ALU.mult))

            for l in range(DEPTH):
                nb = l * LAYER_BLOCKS

                def tile_lo(j):
                    for b in range(first_block(j), first_block(j + 1)):
                        lo_block(nb + b, NARROW_KB * NARROW if j == T_NARROW else BLK)

                def from_turned(j, dst, src):
                    k = TURNED.index(j)
                    dve.wait_ge(tile_turned.sem, tile_turned.at(l, k))
                    dve.tensor_copy(dst, src).then_inc(tile_ch.sem, 1)
                    dve.wait_ge(tile_ch.sem, tile_ch.at(l, k))

                def token_shift(k, c, names):
                    r, n = c.shape[0], c.shape[1]
                    d = shift[0:r, 0:n, :]
                    tt(d[:, :, 1:SEQ], c[:, :, 0:SEQ - 1], c[:, :, 1:SEQ], ALU.subtract)
                    link(ts(d[:, :, 0:1], c[:, :, 0:1], -1.0, None, ALU.mult))
                    for b, (name, i) in enumerate(names):
                        e = stt(c[:, b, :], d[:, b, :], vcol(l, name, i)[0:r], c[:, b, :], ALU.mult, ALU.add)
                    e.then_inc(shifted.sem, 1)
                    dve.wait_ge(shifted.sem, shifted.at(l, k))

                def turned_view(b):
                    return banks(b, 2).rearrange("p t (c n) -> p t c n", c=4)

                if l > 0:
                    start(2 * l, nb)
                else:
                    dve.wait_ge(vecs_loaded, 16)

                tile_lo(T_K)
                for j, dst, name in ((T_R, rT, "mu_r"), (T_K, kT_c, "mu_k"), (T_V, vT_c, "mu_v")):
                    from_turned(j, dst[:, :, :].rearrange("p c (t n) -> p t c n", t=NT), turned_view(4 + 2 * (j % 2)))
                    token_shift(j, dst[:, :, :], [(name, i) for i in range(4)])
                    if j < T_V:
                        tile_lo(j + 2)
                    else:
                        tile_lo(T_NARROW)
                from_turned(T_TAIL, tailT[:, :, :].rearrange("p c (t n) -> p t c n", t=NT), turned_view(6))
                token_shift(3, tailT[:, :, :], [("mu_wl", 0), ("mu_al", 0), ("mu_gl", 0), ("mu_gl", 1)])
                dve.wait_ge(tile_tok.sem, tile_tok.at(l, T_NARROW))
                at, half = ROPE_AT["I"]
                cos, sin = rope_tab[:, :, at:at + half], rope_tab[:, :, at + half:at + 2 * half]
                x1, x2 = tok_n[:, :, 0:half], tok_n[:, :, half:2 * half]
                tmp = [shift[:, k, 0:NT * half].rearrange("p (t f) -> p t f", t=NT) for k in range(4)]
                tt(tmp[0], x1, cos, ALU.mult)
                tt(tmp[1], x2, sin, ALU.mult)
                tt(tmp[2], x2, cos, ALU.mult)
                link(tt(tmp[3], x1, sin, ALU.mult))
                tt(x1, tmp[0], tmp[1], ALU.subtract)
                tt(x2, tmp[2], tmp[3], ALU.add)
                link(ts(wi[:, :, :], tok_n[:, :, I_DIM:I_DIM + I_HEADS], IDX_W_SCALE, None, ALU.mult))
                for d in range(2):
                    e = dve.tensor_copy(ki2[:, :, d, :], tok_n[:, :, 0:I_DIM])
                e.then_inc(tile_rot.sem, 1)
                k = TURNED.index(T_NARROW)
                dve.wait_ge(tile_turned.sem, tile_turned.at(l, k))
                dve.tensor_copy(kiT[:, :], bank(4, SEQ))
                dve.tensor_copy(vrT[:, :], ps[0:MV_LORA, 5, 0:SEQ]).then_inc(tile_ch.sem, 1)
                dve.wait_ge(tile_ch.sem, tile_ch.at(l, k))
                token_shift(4, vrT[:, :].unsqueeze(1), [("mu_vr", 0)])

                if l > 0:
                    dve.wait_ge(v_first_loaded.sem, 16 * l)
                    dve.wait_ge(sv_ready.sem, l)
                    link(tt(kk[:, :, :], kk[:, :, :], vT_c[:, :, :], ALU.subtract))
                    link(tt(kk[:, :, :], kk[:, :, :], kh[:, :, :], ALU.mult))
                    tt(vT_c[:, :, :], vT_c[:, :, :], kk[:, :, :], ALU.add).then_inc(v_mixed.sem, 1)
                    dve.wait_ge(v_mixed.sem, l)
                link(tt(kk[:, :, :], kT_c[:, :, :], vbc(l, "k_k"), ALU.mult))
                tt(kh[:, :, :], kk[:, :, :], kk[:, :, :], ALU.mult).then_inc(sqk_ready.sem, 1)
                dve.wait_ge(w_ready.sem, w_ready.at(l))
                chunks = w_c[:, :, :].rearrange("p b (c n) -> p (b c) n", n=CH)
                tt(d0[:, :].rearrange("p (g n) -> p g n", n=CH), chunks, over_mid(not_start, 16), ALU.mult)
                link(tt(d1[:, :].rearrange("p (g n) -> p g n", n=CH), chunks, over_mid(at_start, 16), ALU.mult))
                link(dve.tensor_tensor_scan(flat(Pd[:, :, :]), d0[:, :], d1[:, :], 0.0, ALU.mult, ALU.add))
                dve.reciprocal(w_c[:, :, :], Pd[:, :, :])
                Pg = Pd[:, :, :].rearrange("p b (c n) -> p (b c) n", n=CH)
                dve.tensor_copy(chunk_decay[:, :].unsqueeze(2), Pg[:, :, CH - 1:CH])
                dve.wait_ge(nrm_ready.sem, nrm_ready.at(l))
                link(ts(inv8[:, :], inv8[:, :], KK_EPS, None, ALU.max))
                dve.reciprocal(inv8[:, :], inv8[:, :]).then_inc(inv_ready.sem, 1)
                dve.wait_ge(a_ready.sem, a_ready.at(l))
                dve.wait_ge(ss_ps.sem, ss_ps.at(l))
                link(stt(kh[:, :, :], a_c[:, :, :], -1.0, vbc(l, "k_a"), ALU.add, ALU.mult))
                link(stt(kh[:, :, :], kh[:, :, :], 1.0, kT_c[:, :, :], ALU.add, ALU.mult))
                tt(KTl[:, :, :], kh[:, :, :], w_c[:, :, :], ALU.mult)
                rg = rT[:, :, :].rearrange("p b (c n) -> p (b c) n", n=CH)
                tt(AR[:, :, 1, :], rg, Pg, ALU.mult)
                link(tt(kh[:, :, :], kh[:, :, :], rT[:, :, :], ALU.mult))
                tt(kh[:, :, :], kh[:, :, :], vbc(l, "r_k"), ALU.mult).then_inc(rkk_ready.sem, 1)
                dve.wait_ge(invb_ps.sem, invb_ps.at(l))
                link(tt(kk[:, :, :], kk[:, :, :], banks(6, 2).rearrange("p t (b n) -> p (t b) n", b=2), ALU.mult))
                kg = kk[:, :, :].rearrange("p b (c n) -> p (b c) n", n=CH)
                stt(AR[:, :, 0, 1:CH], kg[:, :, 1:CH], -1.0, Pg[:, :, 0:CH - 1], ALU.mult, ALU.mult)
                ts(AR[:, :, 0, 0:1], kg[:, :, 0:1], -1.0, None, ALU.mult)
                link(tt(BT[:, :, :], kk[:, :, :], a_c[:, :, :], ALU.mult))
                tt(BT[:, :, :], BT[:, :, :], w_c[:, :, :], ALU.mult).then_inc(ark_ready.sem, 1)

                dve.wait_ge(turned_c.sem, turned_c.at(l, 2))
                if l == 0:
                    dve.wait_ge(v_kept.sem, 16)
                for q in range(4):
                    t, h0 = q // 2, 4 * (q % 2)
                    dve.wait_ge(gram_ps.sem, gram_ps.at(l, q))
                    tt(G[:, t, h0:h0 + 4, :, :].rearrange("p (b o) k n -> p b o (k n)", o=2),
                       banks(4 + 2 * (q % 2), 2).rearrange("p o (b n) -> p b o n", b=2),
                       gram_mask.unsqueeze(1).unsqueeze(1).to_broadcast([P, 2, 2, 4 * CH]), ALU.mult)\
                        .then_inc(gram_ready.sem, 1)
                for lev in range(6):
                    for t in range(NT):
                        k = 2 * lev + t
                        if lev == 0:
                            dve.wait_ge(gram_ready.sem, gram_ready.at(l, 2 * t + 1))
                        tt(Mk[:, t, :, :], G[:, t, :, 0, :], over_mid(level_mask[:, lev, :], 8), ALU.mult)\
                            .then_inc(mk_ready.sem, 1)
                        if lev == 0:
                            dve.wait_ge(mk_ready.sem, mk_ready.at(l, k))
                            tt(Tt[:, t, :, :], Mk[:, t, :, :], over_mid(ident64, 8), ALU.add)
                    for t in range(NT):
                        k = 2 * lev + t
                        if lev == 0:
                            dve.wait_ge(x_ps.sem, x_ps.at(l, k))
                            tt(Tm[:, t, :, :], bank(4 + 2 * t).rearrange("p (h n) -> p h n", h=8),
                               over_mid(ident64, 8), ALU.add).then_inc(t_ready.sem, 1)
                        else:
                            dve.wait_ge(t_ps.sem, t_ps.at(l, k - 2))
                            if lev < 5:
                                tt(Tm[:, t, :, :], Tm[:, t, :, :], bank(4 + 2 * t).rearrange("p (h n) -> p h n", h=8),
                                   ALU.add)
                            tt(Tt[:, t, :, :], Tt[:, t, :, :], bank(5 + 2 * t).rearrange("p (h n) -> p h n", h=8),
                               ALU.add).then_inc(t_ready.sem, 1)
                        dve.wait_ge(t_ready.sem, t_ready.at(l, k))
                dve.memset(S[:, :, :], 0.0)
                dve.memset(S_bd[:, :, :, :], 0.0).then_inc(s_zeroed.sem, 1)
                dve.wait_ge(s_zeroed.sem, s_zeroed.at(l))
                dve.wait_ge(pre_ready.sem, pre_ready.at(l))
                cd = chunk_decay[:, :].rearrange("p (b c) -> p b c", b=4)
                for c in range(NCH):
                    t, rc = c // 2, slice((c % 2) * CH, (c % 2) * CH + CH)
                    if c > 0:
                        dve.wait_ge(w_ps.sem, w_ps.at(l, c - 1))
                        tt(W_sb[rc, :], av[rc, t, :], ps[rc, 4, :], ALU.add).then_inc(w_sbr.sem, 1)
                        link(tt(y_c[rc, t, :], y_c[rc, t, :], ps[rc, 6, :], ALU.add))
                    if c < NCH - 1:
                        dve.wait_ge(s_ps.sem, s_ps.at(l, c))
                        link(tt(S_tmp[:, :, :], S[:, :, :], bank(7, 4 * CH).rearrange("p (b n) -> p b n", b=4),
                                ALU.add))
                        for o in range(2):
                            ro = slice(o * CH, o * CH + CH)
                            tt(S_bd[ro, :, o, :], S_tmp[ro, :, :], last(cd[ro, :, c], CH), ALU.mult)
                        tt(S[:, :, :], S_tmp[:, :, :], last(cd[:, :, c], CH), ALU.mult).then_inc(s_sbr.sem, 1)
                        dve.wait_ge(s_sbr.sem, s_sbr.at(l, c))
                    dve.wait_ge(y_ps.sem, y_ps.at(l, c))
                    tt(y_c[rc, t, :], y_c[rc, t, :], ps[rc, 4, :], ALU.add).then_inc(y_sbr.sem, 1)
                    dve.wait_ge(y_sbr.sem, y_sbr.at(l, c))
                head_norm(l, 0, y_c[:, :, :], yc_c[:, :, :], sq_c[:, :, :], 16, LNX_EPS)
                dve.wait_ge(bonus_ready.sem, bonus_ready.at(l))
                dve.wait_ge(g_ready.sem, g_ready.at(l))
                dve.wait_ge(tok_ready.sem, tok_ready.at(l, 2))
                tt(sq_c[:, :, :].rearrange("p t (h n) -> p (t h) n", h=8),
                   v_tok_c[:, :, :].rearrange("p t (h n) -> p (t h) n", h=8), last(bonus[:, :], W_DIM), ALU.mult)
                link(tt(yc_c[:, :, :], yc_c[:, :, :], over_mid(lnx_sb[:, 0, :], NT), ALU.mult))
                link(tt(yc_c[:, :, :], yc_c[:, :, :], over_mid(lnx_sb[:, 1, :], NT), ALU.add))
                link(tt(yc_c[:, :, :], yc_c[:, :, :], sq_c[:, :, :], ALU.add))
                tt(yc_c[:, :, :], yc_c[:, :, :], g_tok[:, :, :], ALU.mult).then_inc(oc_ready.sem, 1)
                dve.wait_ge(cat_hi.sem, cat_hi.at(l, 0))
                lo_part(flat(cat_l[3][:, :, :, :]), flat(banks(4, 2)), flat(cat_h[3][:, :, :, :]))\
                    .then_inc(cat_lo.sem, 1)

                def rotate(j, tok, kind, heads):
                    dve.wait_ge(tile_tok.sem, tile_tok.at(l, j))
                    rope(tok[:, :, :].rearrange("p t (h n) -> p t h n", h=heads), kind, heads)\
                        .then_inc(tile_rot.sem, 1)

                def gather(j, dst):
                    from_turned(j, dst.rearrange("p c (t n) -> p t c n", t=NT), turned_view(4))

                def index_scores(k0, k1):
                    for k in range(k0, k1):
                        t = k // 4
                        ns = P * (t + 1)
                        dve.wait_ge(relu_ready.sem, relu_ready.at(l, k))
                        for c in range(4):
                            head = 4 * (k % 4) + c
                            src, wh = relu[:, k % 2, c % 2, c // 2, 0:ns], wi[:, t, head:head + 1]
                            if head == 0:
                                e = ts(work[:, t, 0:ns], src, wh, None, ALU.mult)
                            else:
                                e = stt(work[:, t, 0:ns], src, wh, work[:, t, 0:ns], ALU.mult, ALU.add)
                            if c < 3:
                                link(e)
                            else:
                                e.then_inc(relu_used.sem, 1)
                                dve.wait_ge(relu_used.sem, relu_used.at(l, k))

                def top_k(t, rounds, first=False, final=False):
                    ns = P * (t + 1)
                    w = work[:, t, 0:ns]
                    if first:
                        if t == 0:
                            dve.memset(work[0:CH, 0, CH:2 * CH], INADMISSIBLE)
                        else:
                            dve.memset(work[0:CH, 1, 3 * CH:4 * CH], INADMISSIBLE)
                        link(dve.memset(nmax[:, 0:1], 0.0))
                    for _ in range(rounds):
                        link(dve.max(top8[:, :], w))
                        link(dve.match_replace(w, top8[:, :], w, TAKEN))
                    if final:
                        link(ts(keep[:, t, 0:ns], w, TAKEN, BIG, ALU.is_equal, ALU.mult))
                        e = ts(keep[:, t, 0:ns], keep[:, t, 0:ns], -BIG, None, ALU.add)
                        if t == 1:
                            e.then_inc(topk_done.sem, 1)
                        else:
                            link(e)

                tile_lo(T_QI0)
                tile_lo(T_QI1)
                rotate(T_QI0, tok_a[1], "I", 8)
                lo_block(nb + first_block(T_Q0))
                gather(T_QI0, qiT[:, 0:4, :])
                lo_block(nb + first_block(T_Q0) + 1)
                lo_block(nb + first_block(T_Q0) + 2)
                rotate(T_QI1, tok_a[0], "I", 8)
                lo_block(nb + first_block(T_Q0) + 3)
                gather(T_QI1, qiT[:, 4:8, :])
                tile_lo(T_Q1)
                rotate(T_Q0, tok_a[1], "A", 4)
                index_scores(0, 4)
                gather(T_Q0, qT[:, 0:4, :])
                tile_lo(T_K0)
                rotate(T_Q1, tok_a[0], "A", 4)
                index_scores(4, 8)
                gather(T_Q1, qT[:, 4:8, :])
                tile_lo(T_K1)
                rotate(T_K0, tok_a[1], "A", 4)
                top_k(0, 4, first=True)
                gather(T_K0, kT[:, 0:4, :])
                tile_lo(T_V0)
                rotate(T_K1, tok_a[0], "A", 4)
                top_k(0, 4, final=True)
                gather(T_K1, kT[:, 4:8, :])
                tile_lo(T_V1)
                top_k(1, 4, first=True)
                tile_lo(T_BQK)
                top_k(1, 4, final=True)
                tile_lo(T_BV)
                rotate(T_BQK, tok_a[1], "R", 8)
                tile_lo(T_BG)
                gather(T_BQK, bT[:, :, :])

                for t in range(NT):
                    ns = P * (t + 1)
                    dve.wait_ge(att_ps.sem, att_ps.at(l, t))
                    if t == 0:
                        src = flat(banks(0, 2)).rearrange("p (h s) -> p h s", h=8)
                    else:
                        src = flat(banks(4, 4)).rearrange("p (h s) -> p h s", h=8)
                    link(stt(Sx[t][:, :, :], src, A_SCALE, over_mid(keep[:, t, 0:ns], 8), ALU.mult, ALU.add))
                    dve.tensor_reduce(nmax[:, :], Sx[t][:, :, :], AX.X, ALU.max, negate=True).then_inc(masked.sem, 1)
                    dve.wait_ge(exp_ready.sem, exp_ready.at(l, t))
                    link(dve.reciprocal(rsum[:, :], rsum[:, :]))
                    tt(Sx[t][:, :, :], Sx[t][:, :, :], last(rsum[:, :], ns), ALU.mult).then_inc(p_ready.sem, 1)
                    dve.wait_ge(cat_hi.sem, cat_hi.at(l, 1 + t))
                    for q in range(2):
                        e = lo_part(flat(cat_l[q][:, t, :, :]), bank(2 * t + q), flat(cat_h[q][:, t, :, :]))
                    e.then_inc(cat_lo.sem, 1)
                dve.wait_ge(decay_loaded, 16 * (l + 1))
                dve.wait_ge(bs_ps.sem, bs_ps.at(l))
                tt(SB[:, :, :], banks(4, 4)[:, :, 0:384], decay[:, :, :], ALU.mult).then_inc(sb_ready.sem, 1)
                dve.wait_ge(yb_ready.sem, yb_ready.at(l))
                head_norm(l, 1, y_b[:, :, :], yc_b[:, :, :], sq_b[:, :, :], 8, EPS)
                dve.wait_ge(tile_tok.sem, tile_tok.at(l, T_BG))
                tt(yc_b[:, :, :], yc_b[:, :, :], bg[:, :, :], ALU.mult).then_inc(ob_ready.sem, 1)
                dve.wait_ge(cat_hi.sem, cat_hi.at(l, 3))
                lo_part(flat(cat_l[2][:, :, :, :]), flat(banks(4, 2)), flat(cat_h[2][:, :, :, :]))\
                    .then_inc(cat_lo.sem, 1)

                for cb in range(4):
                    n0 = nb + OUT_B0 + 4 * cb
                    lo_block(n0)
                    lo_block(n0 + 1)
                    if cb > 0:
                        residual(resid_out, l, cb - 1)
                    lo_block(n0 + 2)
                    lo_block(n0 + 3)
                    if cb > 0:
                        norm_lo(2 * l + 1, cb - 1)

                def ffn(i, first):
                    n0 = nb + FFN_B0 + i * 8
                    g = i * 1 + (l * FT)

                    def lo_at(b):
                        dve.wait_ge(hi_ready, n0 + (b + 1))
                        lo_part(w_lo[:, b % 2, :], raw[:, (nb + FFN_B0 + b) % 4, :], w_hi[:, b % 2, :])\
                            .then_inc(lo_ready, 1)

                    if first:
                        start(2 * l + 1, n0)
                    else:
                        lo_at(0)
                        lo_at(1)
                        product(n0, g)
                        lo_at(2)
                        lo_at(3)
                        turned_lo(i - 1, g)
                    for b in range(4, 8):
                        lo_at(b)

                def product(done, g):
                    dve.wait_ge(mm_done, done)
                    dve.wait_ge(silu_ready.sem, g)
                    for t in range(NT):
                        e = stt(ff_act[:, t, :], bank(2 + t), rstd[:, t:t + 1], ff_act[:, t, :], ALU.mult, ALU.mult)
                    e.then_inc(ffa_ready.sem, 1)

                def turned_lo(i, g):
                    dve.wait_ge(ff_hi_ready.sem, g)
                    for t in range(NT):
                        e = lo_part(flat(ff_lo[:, t, :, :])[:, bass.ds(i * 512, 512)], bank(4 + t),
                                    flat(ff_hi[:, t, :, :])[:, bass.ds(i * 512, 512)])
                    e.then_inc(ff_lo_ready.sem, 1)

                ffn(0, True)
                with dve.Fori(1, FT) as i:
                    ffn(i, False)
                product(nb + DOWN_B0, FT * (l + 1))
                turned_lo(FT - 1, FT * (l + 1))

                for cb in range(4):
                    n0 = nb + DOWN_B0 + DOWN_PER * cb
                    for b in range(DOWN_PER):
                        lo_block(n0 + b)
                        if b == 1 and cb > 0:
                            residual(resid_down, l, cb - 1)
                        if b == 4 and cb > 0 and l < DEPTH - 1:
                            norm_lo(2 * l + 2, cb - 1)
            residual(resid_down, DEPTH - 1, 3)
            var(2 * DEPTH)
            invert_std(2 * DEPTH)
            dve.wait_ge(rstd_ready, 2 * DEPTH + 1)
            dve.wait_ge(gain_loaded, 16)
            for k in range(2 * NT):
                t, cols = k // 2, slice((k % 2) * (D // 2), (k % 2 + 1) * (D // 2))
                stt(x[:, t, cols], x[:, t, cols], rstd[:, t:t + 1], gain_row[:, cols], ALU.mult, ALU.mult)\
                    .then_inc(out_ready, 1)

        @block.tensor
        def _(pe):
            mm, turn = pe.matmul, pe.transpose

            def three(acc, st_hi, st_lo, mv_hi, mv_lo, start, stop):
                mm(acc, st_hi, mv_hi, start=start, stop=False)
                mm(acc, st_hi, mv_lo, start=False, stop=False)
                return mm(acc, st_lo, mv_hi, start=False, stop=stop)

            def mm_block(n, s2, hi, lo, k0, nk, w, b0, first, final):
                pe.wait_ge(lo_ready, n)
                for k in range(nk):
                    for t in range(NT):
                        e = three(ps[:, b0 + t, 0:w], hi[:, t, k0 + k, :], lo[:, t, k0 + k, :],
                                  w_hi[:, s2, k * w:(k + 1) * w], w_lo[:, s2, k * w:(k + 1) * w],
                                  first and k == 0, final and k == nk - 1)
                e.then_inc(mm_done, 1)

            def turn_x(m, q):
                if m == 0:
                    pe.wait_ge(x_loaded[q], 16)
                else:
                    r = resid_down if m % 2 == 0 else resid_out
                    pe.wait_ge(r.sem, r.at((m - 1) // 2, q))
                if q >= 2:
                    pe.wait_ge(act_lo_ready, 4 * m + q - 1)
                for t in range(NT):
                    for c in range(KB):
                        k = KB * q + c
                        e = turn(ps[:, 4 + 2 * (q % 2) + t, c * P:(c + 1) * P], x[:, t, k * P:(k + 1) * P], ident)
                e.then_inc(x_turned, 1)

            def x_split(m, q):
                pe.wait_ge(act_lo_ready, 4 * m + q + 1)

            pe.wait_ge(consts_loaded, 32)
            for l in range(DEPTH):
                nb = l * LAYER_BLOCKS

                def tile_blocks(j, b_from, b_to):
                    w, nk = (NARROW, NARROW_KB) if j == T_NARROW else (TW, KB)
                    if b_from == 0:
                        if j >= 2:
                            pe.wait_ge(tile_tok.sem, tile_tok.at(l, j - 2))
                        elif l > 0:
                            pe.wait_ge(resid_down.sem, resid_down.at(l - 1, 2 + j))
                    for b in range(b_from, b_to):
                        n = nb + first_block(j) + b
                        mm_block(n + 1, n % 2, act_hi, act_lo, b * nk, nk, w, 2 * (j % 2), b == 0, b == KT // nk - 1)

                def tile_mm(j):
                    tile_blocks(j, 0, KT // (NARROW_KB if j == T_NARROW else KB))

                def turn_tile(j, src, b):
                    k = TURNED.index(j)
                    if j in ROTATED:
                        pe.wait_ge(tile_rot.sem, tile_rot.at(l, ROTATED.index(j)))
                    else:
                        pe.wait_ge(tile_tok.sem, tile_tok.at(l, j))
                    if k >= 1:
                        pe.wait_ge(tile_ch.sem, tile_ch.at(l, k - 1))
                    for t in range(NT):
                        for c in range(4):
                            e = turn(ps[:, b + t, c * P:(c + 1) * P], src[:, t, c * P:(c + 1) * P], ident)
                    e.then_inc(tile_turned.sem, 1)

                if l == 0:
                    turn_x(0, 0)
                    turn_x(0, 1)
                    for b in range(2):
                        x_split(0, b)
                        tile_blocks(T_R, b, b + 1)
                        turn_x(0, b + 2)
                    x_split(0, 2)
                    tile_blocks(T_R, 2, 3)
                    x_split(0, 3)
                else:
                    x_split(2 * l, 2)
                    tile_blocks(T_R, 0, 1)
                    turn_x(2 * l, 3)
                    tile_blocks(T_R, 1, 3)
                    x_split(2 * l, 3)
                tile_blocks(T_R, 3, 4)
                tile_blocks(T_K, 0, 3)
                turn_tile(T_R, tok_c[0], 4)
                tile_blocks(T_K, 3, 4)
                tile_blocks(T_V, 0, 3)
                turn_tile(T_K, tok_c[1], 6)
                tile_blocks(T_V, 3, 4)
                tile_blocks(T_TAIL, 0, 3)
                turn_tile(T_V, tok_c[0], 4)
                tile_blocks(T_TAIL, 3, 4)
                tile_mm(T_NARROW)
                turn_tile(T_TAIL, tok_c[1], 6)
                pe.wait_ge(tile_rot.sem, tile_rot.at(l, 0))
                pe.wait_ge(tile_ch.sem, tile_ch.at(l, TURNED.index(T_TAIL)))
                for t in range(NT):
                    turn(ps[:, 4, t * P:(t + 1) * P], flat(ki2[:, t, :, :]), ident)
                for t in range(NT):
                    e = turn(ps[0:MV_LORA, 5, t * P:(t + 1) * P], tok_n[:, t, I_DIM + I_HEADS:NARROW], ident)
                e.then_inc(tile_turned.sem, 1)

                pe.wait_ge(c_params, 96 * (l + 1))
                pe.wait_ge(lora_in.sem, lora_in.at(l))

                def lora(b0, w_sb, src, rows):
                    for b in range(4):
                        e = mm(flat(banks(b0, 2))[:, b * SEQ:(b + 1) * SEQ], w_sb[0:rows, b * P:(b + 1) * P], src,
                               start=True, stop=True)
                    return e

                lora(6, alb_sb, tailT[0:AAA_LORA, 1, :], AAA_LORA).then_inc(za_ps.sem, 1)
                pe.wait_ge(tile_ch.sem, tile_ch.at(l, TURNED.index(T_NARROW)))
                lora(4, wlb_sb, tailT[0:DECAY_LORA, 0, :], DECAY_LORA).then_inc(zw_ps.sem, 1)
                pe.wait_ge(a_ready.sem, a_ready.at(l))
                for t in range(NT):
                    for k in range(2):
                        e = mm(bank(6 + t), tailT[:, 2 + k, t * P:(t + 1) * P], glb_sb[:, k, :],
                               start=(k == 0), stop=(k == 1))
                e.then_inc(g_ps.sem, 1)
                pe.wait_ge(w_ready.sem, w_ready.at(l))
                if l > 0:
                    pe.wait_ge(shifted.sem, shifted.at(l, 4))
                    lora(4, vlb_sb, vrT[:, :], MV_LORA).then_inc(zv_ps.sem, 1)
                    pe.wait_ge(sv_ready.sem, l)
                pe.wait_ge(sqk_ready.sem, sqk_ready.at(l))
                for b in range(4):
                    e = mm(ps[0:8, 4, 0:SEQ], headmask[:, b, :], kh[:, b, :], start=(b == 0), stop=(b == 3))
                e.then_inc(ss_ps.sem, 1)
                pe.wait_ge(inv_ready.sem, inv_ready.at(l))
                pe.wait_ge(g_ready.sem, g_ready.at(l))
                for b in range(4):
                    e = mm(flat(banks(6, 2))[:, b * SEQ:(b + 1) * SEQ], hmt_sb[:, b * P:(b + 1) * P], inv8[:, :],
                           start=True, stop=True)
                e.then_inc(invb_ps.sem, 1)
                pe.wait_ge(ark_ready.sem, ark_ready.at(l))
                for n, (src, b0) in enumerate(((BT, 4), (KTl, 6), (vT_c, 4))):
                    if n == 2:
                        pe.wait_ge(tok_ready.sem, tok_ready.at(l, 0))
                        if l > 0:
                            pe.wait_ge(v_mixed.sem, l)
                    for t in range(NT):
                        for b in range(4):
                            e = turn(ps[:, b0 + t, b * P:(b + 1) * P], src[:, b, t * P:(t + 1) * P], ident)
                    e.then_inc(turned_c.sem, 1)
                pe.wait_ge(rkk_ready.sem, rkk_ready.at(l))
                pe.wait_ge(tok_ready.sem, tok_ready.at(l, 1))
                for t in range(NT):
                    for b in range(4):
                        e = mm(ps[:, 6, 8 * t:8 * t + 8], kh[:, b, t * P:(t + 1) * P], headmask[:, b, :],
                               start=(b == 0), stop=(b == 3))
                e.then_inc(bonus_ps.sem, 1)

                def rows(o):
                    return slice(o * CH, o * CH + CH)

                for q in range(4):
                    t, h0 = q // 2, 4 * (q % 2)
                    if q == 0:
                        pe.wait_ge(tok_ready.sem, tok_ready.at(l, 2))
                    elif q == 1:
                        pe.wait_ge(bonus_ready.sem, bonus_ready.at(l))
                    else:
                        pe.wait_ge(gram_ready.sem, gram_ready.at(l, q - 2))
                    for h in range(h0, h0 + 4):
                        b, o = h // 2, h % 2
                        for c in range(2):
                            c4 = 2 * t + c
                            bk, col = 4 + 2 * (q % 2) + o, 256 * (b % 2)
                            for src, at in ((BT, 0), (KTl, 128)):
                                e = mm(ps[rows(c), bk, col + at:col + at + 128],
                                       src[rows(o), b, c4 * CH:(c4 + 1) * CH],
                                       AR[rows(o), 4 * b + c4, :, :].rearrange("p k n -> p (k n)"),
                                       start=True, stop=True)
                    e.then_inc(gram_ps.sem, 1)
                for lev in range(6):
                    for t in range(NT):
                        k = 2 * lev + t
                        pe.wait_ge(mk_ready.sem, mk_ready.at(l, k))
                        if lev == 0:
                            pe.wait_ge(gram_ready.sem, gram_ready.at(l, 3))
                        else:
                            pe.wait_ge(t_ready.sem, t_ready.at(l, k - 2))
                        for h in range(8):
                            for c in range(2):
                                rhs = ident[rows(c), c * CH:(c + 1) * CH] if lev == 0 else Tm[rows(c), t, h, :]
                                e = mm(ps[rows(c), 4 + 2 * t, h * CH:(h + 1) * CH], Mk[rows(c), t, h, :], rhs,
                                       start=True, stop=True)
                        e.then_inc(x_ps.sem, 1)
                    if lev == 0:
                        continue
                    for t in range(NT):
                        k = 2 * lev + t
                        pe.wait_ge(x_ready.sem, x_ready.at(l, k - 2))
                        for h in range(8):
                            for c in range(2):
                                if lev < 5:
                                    mm(ps[rows(c), 4 + 2 * t, h * CH:(h + 1) * CH], Tt[rows(c), t, h, :],
                                       Xm[rows(c), t, h, :], start=True, stop=True)
                                e = mm(ps[rows(c), 5 + 2 * t, h * CH:(h + 1) * CH], Xm[rows(c), t, h, :],
                                       Tt[rows(c), t, h, :], start=True, stop=True)
                        e.then_inc(t_ps.sem, 1)
                pe.wait_ge(t_ready.sem, t_ready.at(l, 11))
                pe.wait_ge(s_zeroed.sem, s_zeroed.at(l))
                for t in range(NT):
                    for h in range(8):
                        for c in range(2):
                            rc, cols = rows(c), slice(h * CH, (h + 1) * CH)
                            mm(ps[rc, 4 + t, cols], G[rc, t, h, 2, :], v_tok_c[rc, t, cols], start=True, stop=True)
                            e = mm(ps[rc, 6 + t, cols], G[rc, t, h, 3, :], v_tok_c[rc, t, cols], start=True, stop=True)
                e.then_inc(pre_ps.sem, 1)
                pe.wait_ge(pre_ready.sem, pre_ready.at(l))
                for c4 in range(NCH):
                    t, c = c4 // 2, c4 % 2
                    rc = rows(c)
                    if c4 > 0:
                        pe.wait_ge(s_sbr.sem, s_sbr.at(l, c4 - 1))
                        for kind, bk in ((0, 4), (1, 6)):
                            for b in range(4):
                                e = mm(ps[rc, bk, b * P:(b + 1) * P], AR[:, 4 * b + c4, kind, :],
                                       S_bd[:, b, :, :].rearrange("p o n -> p (o n)"), start=True, stop=True)
                        e.then_inc(w_ps.sem, 1)
                        pe.wait_ge(w_sbr.sem, w_sbr.at(l, c4 - 1))
                    for h in range(8):
                        cols = slice(h * CH, (h + 1) * CH)
                        src = W_sb[rc, cols] if c4 > 0 else av[rc, t, cols]
                        e = mm(ps[rc, 5, cols], Tt[rc, t, h, :], src, start=True, stop=True)
                    e.then_inc(u_ps.sem, 1)
                    pe.wait_ge(u_sbr.sem, u_sbr.at(l, c4))
                    if c4 < NCH - 1:
                        for h in range(8):
                            b, o, cols = h // 2, h % 2, slice(h * CH, (h + 1) * CH)
                            mm(ps[rows(o), 7, b * CH:(b + 1) * CH], b_tok[rc, t, cols], U_sb[rc, cols],
                               start=True, stop=False)
                            e = mm(ps[rows(o), 7, b * CH:(b + 1) * CH], k_tok[rc, t, cols], v_tok_c[rc, t, cols],
                                   start=False, stop=True)
                        e.then_inc(s_ps.sem, 1)
                    for h in range(8):
                        cols = slice(h * CH, (h + 1) * CH)
                        e = mm(ps[rc, 4, cols], G[rc, t, h, 1, :], U_sb[rc, cols], start=True, stop=True)
                    e.then_inc(y_ps.sem, 1)
                pe.wait_ge(oc_ready.sem, oc_ready.at(l))
                for t in range(NT):
                    for b in range(4):
                        e = turn(ps[:, 4 + t, b * P:(b + 1) * P], yc_c[:, t, b * P:(b + 1) * P], ident)
                e.then_inc(oc_turned.sem, 1)

                def index_mm(k0, k1):
                    for k in range(k0, k1):
                        t = k // 4
                        if k >= k0 + 2:
                            pe.wait_ge(relu_ready.sem, relu_ready.at(l, k - 2))
                        for c in range(4):
                            o, pair = c % 2, c // 2
                            e = mm(ps[:, 4 + 2 * (k % 2) + o, 256 * pair:256 * pair + P * (t + 1)],
                                   qiT[rows(o), 2 * (k % 4) + pair, t * P:(t + 1) * P],
                                   kiT[rows(o), 0:P * (t + 1)], start=True, stop=True)
                        e.then_inc(score_ps.sem, 1)
                    pe.wait_ge(relu_ready.sem, relu_ready.at(l, k1 - 1))

                tile_mm(T_QI0)
                tile_blocks(T_QI1, 0, 4)
                pe.wait_ge(cat_lo.sem, cat_lo.at(l, 0))
                tile_blocks(T_Q0, 0, 1)
                turn_tile(T_QI0, tok_a[1], 4)
                tile_blocks(T_Q0, 1, 4)
                turn_tile(T_QI1, tok_a[0], 4)
                tile_mm(T_Q1)
                pe.wait_ge(tile_ch.sem, tile_ch.at(l, TURNED.index(T_QI1)))
                index_mm(0, 4)
                turn_tile(T_Q0, tok_a[1], 4)
                tile_mm(T_K0)
                pe.wait_ge(tile_ch.sem, tile_ch.at(l, TURNED.index(T_Q0)))
                index_mm(4, 8)
                turn_tile(T_Q1, tok_a[0], 4)
                tile_mm(T_K1)
                turn_tile(T_K0, tok_a[1], 4)
                tile_mm(T_V0)
                turn_tile(T_K1, tok_a[0], 4)
                tile_mm(T_V1)
                tile_mm(T_BQK)
                tile_mm(T_BV)
                tile_mm(T_BG)
                turn_tile(T_BQK, tok_a[1], 4)

                pe.wait_ge(topk_done.sem, topk_done.at(l))
                pe.wait_ge(tile_tok.sem, tile_tok.at(l, T_BG))
                pe.wait_ge(tile_ch.sem, tile_ch.at(l, TURNED.index(T_BQK)))
                for h in range(A_HEADS):
                    e = mm(flat(banks(0, 2))[:, h * P:(h + 1) * P], qT[:, h, 0:P], kT[:, h, 0:P], start=True, stop=True)
                e.then_inc(att_ps.sem, 1)
                for h in range(A_HEADS):
                    e = mm(flat(banks(4, 4))[:, h * SEQ:(h + 1) * SEQ], qT[:, h, P:SEQ], kT[:, h, :],
                           start=True, stop=True)
                e.then_inc(att_ps.sem, 1)
                for t in range(NT):
                    pe.wait_ge(p_ready.sem, p_ready.at(l, t))
                    for h in range(A_HEADS):
                        for s in range(t + 1):
                            dst = flat(banks(4, 4))[:, (2 * h + s) * P:(2 * h + s + 1) * P] if t else \
                                flat(banks(2, 2))[:, h * P:(h + 1) * P]
                            e = turn(dst, Sx[t][:, h, s * P:(s + 1) * P], ident)
                    e.then_inc(p_turned.sem, 1)
                    pe.wait_ge(pT_ready.sem, pT_ready.at(l, t))
                    for h in range(A_HEADS):
                        for s in range(t + 1):
                            e = mm(flat(banks(2 * t, 2))[:, h * P:(h + 1) * P], v_tok[:, s, h * P:(h + 1) * P],
                                   PT[t][:, h, s, :], start=(s == 0), stop=(s == t))
                    e.then_inc(pv_ps.sem, 1)
                for h in range(R_HEADS):
                    b, o = h // 2, h % 2
                    mm(ps[:, 4 + h, 0:256], bT[rows(o), 2 + b, 0:P], bT[rows(o), b, :], start=True, stop=True)
                    e = mm(ps[:, 4 + h, 256:384], bT[rows(o), 2 + b, P:SEQ], bT[rows(o), b, P:SEQ],
                           start=True, stop=True)
                e.then_inc(bs_ps.sem, 1)
                pe.wait_ge(sb_ready.sem, sb_ready.at(l))
                pe.wait_ge(cat_lo.sem, cat_lo.at(l, 1))
                for h in range(R_HEADS):
                    cols = slice(h * R_V, (h + 1) * R_V)
                    mm(ps[:, 0, cols], SB[:, h, 0:P], bv[:, 0, cols], start=True, stop=True)
                    mm(ps[:, 1, cols], SB[:, h, P:2 * P], bv[:, 0, cols], start=True, stop=False)
                    e = mm(ps[:, 1, cols], SB[:, h, 2 * P:3 * P], bv[:, 1, cols], start=False, stop=True)
                e.then_inc(yb_ps.sem, 1)
                pe.wait_ge(ob_ready.sem, ob_ready.at(l))
                for t in range(NT):
                    for b in range(4):
                        e = turn(ps[:, 4 + t, b * P:(b + 1) * P], yc_b[:, t, b * P:(b + 1) * P], ident)
                e.then_inc(ob_turned.sem, 1)

                pe.wait_ge(cat_lo.sem, cat_lo.at(l, 3))
                for cb in range(4):
                    if cb >= 2:
                        pe.wait_ge(resid_out.sem, resid_out.at(l, cb - 2))
                    for b in range(4):
                        if cb > 0 and b == 2:
                            turn_x(2 * l + 1, cb - 1)
                        n = nb + OUT_B0 + 4 * cb + b
                        mm_block(n + 1, n % 2, cat_h[b], cat_l[b], 0, KB, TW, 2 * (cb % 2), b == 0, b == 3)

                def turn_product(i, g):
                    pe.wait_ge(ffa_ready.sem, g)
                    for t in range(NT):
                        for c in range(4):
                            e = turn(ps[:, 4 + t, c * P:(c + 1) * P], ff_act[:, t, c * P:(c + 1) * P], ident)
                    e.then_inc(ffa_turned.sem, 1)

                def ffn(i, first):
                    n0 = nb + FFN_B0 + i * 8
                    g = i * 1 + (l * FT)
                    if first:
                        x_split(2 * l + 1, 2)
                        pe.wait_ge(resid_out.sem, resid_out.at(l, 2))
                    else:
                        pe.wait_ge(silu_ready.sem, g)
                    for b in range(8):
                        if b == 1 and first:
                            turn_x(2 * l + 1, 3)
                        if b == 3 and first:
                            x_split(2 * l + 1, 3)
                        if b == 2 and not first:
                            turn_product(i, g)
                        mm_block(n0 + (b + 1), b % 2, act_hi, act_lo, KB * (b % 4), KB, TW, 2 * (b // 4),
                                 b % 4 == 0, b % 4 == 3)

                ffn(0, True)
                with pe.Fori(1, FT) as i:
                    ffn(i, False)
                turn_product(FT - 1, FT * (l + 1))
                pe.wait_ge(ff_lo_ready.sem, FT * (l + 1))

                for cb in range(4):
                    if cb >= 2:
                        pe.wait_ge(resid_down.sem, resid_down.at(l, cb - 2))
                    for b in range(DOWN_PER):
                        if b == 3 and cb > 0 and l < DEPTH - 1:
                            turn_x(2 * l + 2, cb - 1)
                        n = nb + DOWN_B0 + DOWN_PER * cb + b
                        mm_block(n + 1, n % 2, ff_hi, ff_lo, KB * b, KB, TW, 2 * (cb % 2), b == 0, b == DOWN_PER - 1)


def _constants():
    pos = np.arange(SEQ, dtype=np.float32)
    tabs = []
    for half, theta in ((A_HALF, 500000.0), (I_HALF, 500000.0), (R_HALF, 10000.0)):
        freqs = np.power(np.float32(theta), -np.arange(half, dtype=np.float32) / np.float32(half))
        ang = pos[:, None] * freqs[None, :].astype(np.float32)
        tabs += [np.cos(ang), np.sin(ang)]
    rope = np.concatenate(tabs, axis=1).reshape(NT, P, -1).transpose(1, 0, 2).reshape(P, -1)
    p = np.arange(P)
    headmask = np.zeros((P, 4, 8), np.float32)
    for b in range(4):
        headmask[p, b, 2 * b + p // W_DIM] = 1
    s, t = p[:, None] % CH, np.arange(CH)[None, :]
    strict, inclusive = s < t, s <= t
    gram = np.concatenate([strict, inclusive, strict, inclusive], axis=1)
    level = [(s >> (k + 1) == t >> (k + 1)) & (s >> k & 1 == 0) & (t >> k & 1 == 1) for k in range(6)]
    start = np.broadcast_to(t == 0, (P, CH))
    consts = np.concatenate([np.eye(P), rope, headmask.reshape(P, -1), gram, *level, s == t, ~start, start],
                            axis=1).astype(np.float32)
    assert consts.shape == (P, N_CONST)
    log_g = np.log1p(-np.power(2.0, -5.0 - np.arange(R_HEADS)))
    m, n = p[:, None], np.arange(SEQ)[None, :]
    whole = np.where(n >= m, 1.0, 0.0) * np.exp(np.maximum(n - m, 0)[None] * log_g[:, None, None])
    decay = np.concatenate([whole, whole[:, :, 0:P]], axis=2).transpose(1, 0, 2) * R_QK ** -0.5
    headmask_t = headmask.transpose(2, 1, 0).reshape(8, 4 * P)
    return consts, decay.reshape(P, -1).astype(np.float32), np.ascontiguousarray(headmask_t)


def _blocks(w, kb=KB):
    k, n = w.shape
    return w.reshape(k // (kb * P), kb, P, n).transpose(0, 2, 1, 3).reshape(-1, P, kb * n)


def _stream(w_in, w_in_vres, w_out, w_gate_up, w_down):
    s = np.zeros((N_BLOCKS, P, BLK), w_in.dtype)
    full = [(T_R, C0), (T_K, C0 + C_W), (T_V, C0 + 2 * C_W), (T_QI0, QI0), (T_QI1, QI0 + TW), (T_Q0, Q0),
            (T_Q1, Q0 + TW), (T_K0, K0), (T_K1, K0 + TW), (T_V0, V0), (T_V1, V0 + TW), (T_BQK, BQ0),
            (T_BV, BV0), (T_BG, BG0)]
    for l in range(DEPTH):
        nb = l * LAYER_BLOCKS
        for j, c in full:
            s[nb + first_block(j):nb + first_block(j + 1)] = _blocks(w_in[l][:, c:c + TW])
        tail = np.zeros((D, TW), w_in.dtype)
        tail[:, 0:DECAY_LORA] = w_in[l][:, WL0:AL0]
        tail[:, P:P + AAA_LORA] = w_in[l][:, AL0:GL0]
        tail[:, 2 * P:] = w_in[l][:, GL0:GL0 + GATE_LORA]
        s[nb + first_block(T_TAIL):nb + first_block(T_NARROW)] = _blocks(tail)
        narrow = np.zeros((D, NARROW), w_in.dtype)
        narrow[:, 0:I_DIM + I_HEADS] = w_in[l][:, KI0:BQ0]
        if l > 0:
            narrow[:, I_DIM + I_HEADS:] = w_in_vres[l - 1]
        s[nb + first_block(T_NARROW):nb + first_block(T_QI0), :, 0:NARROW_KB * NARROW] = _blocks(narrow, NARROW_KB)
        for c in range(4):
            cols = slice(c * TW, (c + 1) * TW)
            s[nb + OUT_B0 + 4 * c:nb + OUT_B0 + 4 * c + 4] = _blocks(w_out[l][:, cols])
            s[nb + DOWN_B0 + DOWN_PER * c:nb + DOWN_B0 + DOWN_PER * (c + 1)] = _blocks(w_down[l][:, cols])
        for f in range(FT):
            for part in range(2):
                at = nb + FFN_B0 + 8 * f + 4 * part
                c = part * D_FF + f * TW
                s[at:at + 4] = _blocks(w_gate_up[l][:, c:c + TW])
    return s.reshape(N_BLOCKS * P, BLK)


def _vectors(i):
    v = np.zeros((P, DEPTH, N_VEC), np.float32)

    def put(l, name, a, rows=P):
        at, n = VEC[name]
        v[0:rows, l, at:at + n] = np.asarray(a).reshape(n, rows).T

    for l in range(DEPTH):
        mu = i["rwkv_mu"][l]
        o = 3 * C_W
        put(l, "mu_r", mu[0:C_W])
        put(l, "mu_k", mu[C_W:2 * C_W])
        put(l, "mu_v", mu[2 * C_W:o])
        put(l, "mu_wl", mu[o:o + DECAY_LORA], DECAY_LORA)
        put(l, "mu_al", mu[o + DECAY_LORA:o + DECAY_LORA + AAA_LORA], AAA_LORA)
        put(l, "mu_gl", mu[o + DECAY_LORA + AAA_LORA:])
        put(l, "w0", i["rwkv_w0"][l])
        put(l, "a0", i["rwkv_a0"][l])
        put(l, "k_k", i["rwkv_k_k"][l])
        put(l, "k_a", i["rwkv_k_a"][l])
        put(l, "r_k", i["rwkv_r_k"][l])
        if l > 0:
            put(l, "mu_vr", i["rwkv_mu_vres"][l - 1], MV_LORA)
            put(l, "v0", i["rwkv_v0"][l - 1])
    return v.reshape(P, DEPTH * N_VEC)


def kernel(**inputs):
    import concourse.bacc as _bacc
    from concourse.bass_utils import run_bass_kernel_spmd as _run

    i = {k: np.asarray(v) for k, v in inputs.items()}
    consts, decay, headmask_t = _constants()
    gain_cols = np.concatenate([g.reshape(KT, P).T for l in range(DEPTH)
                                for g in (i["norm_mix_g"][l], i["norm_ffn_g"][l])], axis=1)
    arrays = {
        "x_in": i["x"].reshape(SEQ, D),
        "stream": _stream(i["w_in"], i["w_in_vres"], i["w_out"], i["w_gate_up"], i["w_down"]),
        "consts": consts, "decay_in": decay, "headmask_t": headmask_t, "vecs": _vectors(i),
        "wlb": i["rwkv_w_lora_b"], "alb": i["rwkv_a_lora_b"], "vlb": i["rwkv_v_lora_b"][0],
        "glb": i["rwkv_g_lora_b"],
        "lnx": np.concatenate([i["rwkv_lnx_g"], i["rwkv_lnx_b"]], axis=1),
        "gain_cols": gain_cols, "final_gain": i["final_norm_g"].reshape(1, D),
    }
    nc = _bacc.Bacc("TRN2", target_bir_lowering=False, num_devices=1, dynamic_dma_scratch_size=8192)
    args, maps = {}, {}
    for name, a in arrays.items():
        a = np.ascontiguousarray(a)
        maps[name + "_dram"] = a
        args[name] = nc.dram_tensor(name + "_dram", a.shape, mybir.dt.from_np(a.dtype), kind="ExternalInput").ap()
    v_keep = nc.dram_tensor("v_keep_dram", (P, 4 * SEQ), F32, kind="Internal").ap()
    out = nc.dram_tensor("out_dram", (SEQ, D), F32, kind="ExternalOutput").ap()
    build(nc, out=out, v_keep=v_keep, **args)
    r = _run(nc, [maps], core_ids=[0])
    return r.results[0]["out_dram"].reshape(1, SEQ, D)
```

```python
from contextlib import ExitStack

import numpy as np
import concourse.bass as bass
from concourse import mybir

F32 = mybir.dt.float32
F32R = mybir.dt.float32r
ACT = mybir.ActivationFunctionType
ALU = mybir.AluOpType
AX = mybir.AxisListType

P = 128
SEQ, D, DEPTH = 256, 2048, 2
NT = SEQ // P
CH = 64
NCH = SEQ // CH
KT = D // P
TW = 512
KB = 4
BLK = KB * TW

A_HEADS, A_DIM = 8, 128
I_HEADS, I_DIM = 16, 64
R_HEADS, R_QK, R_V = 4, 64, 128
W_HEADS, W_DIM = 8, 64
TOPK = 64
A_HALF, I_HALF, R_HALF = A_DIM // 8, I_DIM // 8, R_QK // 2
A_W, I_W, C_W = A_HEADS * A_DIM, I_HEADS * I_DIM, W_HEADS * W_DIM
DECAY_LORA, AAA_LORA, GATE_LORA, MV_LORA = 96, 96, 256, 64
D_FF = 5632
FT = D_FF // TW
FK = D_FF // P
IDX_W_SCALE = float((I_HEADS * I_DIM) ** -0.5)
A_SCALE = float(A_DIM ** -0.5)
EXP_M_HALF = float(np.exp(-0.5))
EPS, LNX_EPS, KK_EPS = 1e-5, 64e-5, 1e-12
BIG = 1e30
INADMISSIBLE, TAKEN = -1e38, -3e38

Q0, K0, V0 = 0, A_W, 2 * A_W
QI0 = 3 * A_W
KI0 = QI0 + I_W
WI0 = KI0 + I_DIM
BQ0 = WI0 + I_HEADS
BV0 = BQ0 + 2 * R_HEADS * R_QK
BG0 = BV0 + R_HEADS * R_V
C0 = BG0 + R_HEADS * R_V
WL0 = C0 + 3 * C_W
AL0 = WL0 + DECAY_LORA
GL0 = AL0 + AAA_LORA

(T_R, T_K, T_V, T_TAIL, T_NARROW, T_V0, T_BV, T_BG, T_V1, T_BQK, T_QI0, T_QI1, T_Q0, T_K0,
 T_Q1, T_K1) = range(16)
N_TILES = 16
NARROW = I_DIM + I_HEADS
NARROW_KB = 8
TURNED = (T_R, T_K, T_V, T_TAIL, T_NARROW, T_BQK, T_QI0, T_QI1, T_Q0, T_K0, T_Q1, T_K1)
ROTATED = TURNED[TURNED.index(T_NARROW):]

def first_block(j):
    return KB * j if j <= T_NARROW else KB * (j - 1) + KT // NARROW_KB

IN_BLOCKS = first_block(N_TILES)
OUT_B0 = IN_BLOCKS
FFN_B0 = OUT_B0 + 4 * (KT // KB)
DOWN_B0 = FFN_B0 + 2 * FT * (KT // KB)
DOWN_PER = FK // KB
LAYER_BLOCKS = DOWN_B0 + 4 * DOWN_PER
N_BLOCKS = DEPTH * LAYER_BLOCKS

Q_A0, Q_A1, Q_B, Q_C = range(4)
OUT_ORDER = [(0, Q_C), (0, Q_B), (0, Q_A0), (1, Q_C), (1, Q_B), (1, Q_A0), (0, Q_A1), (1, Q_A1)] + \
            [(cb, q) for cb in (2, 3) for q in (Q_C, Q_B, Q_A0, Q_A1)]
OUT_DONE = [1 + max(i for i, (c, _) in enumerate(OUT_ORDER) if c == cb) for cb in range(4)]

UPTO, _at = {}, 0
for _name, _n in ([("start", 0), ("keys0", 2), ("keys1", 2), ("keys", 4), ("decay", 2), ("gate", 4),
                   ("norm1", 4), ("rate1", 4), ("rate2", 4), ("rate3", 4), ("rate4", 4), ("rate5", 4), ("turned", 2), ("gram", 2), ("level0", 2)]
                  + [("turn_t1", 2), ("level1", 1)]
                  + [(f"{s}{k}", n) for k in range(2, 6) for s, n in (("turn_t", 1), ("level", 2))]
                  + [("inverse", 2), ("pre", 1)]
                  + [(f"{s}{c}", 1) for c in range(NCH) for s in "wus" if (s != "w" or c) and (s != "s" or c < 3)]):
    _at += _n
    UPTO[_name] = _at
UPTO.update(out1=76, out2=80, out3=84, out4=91, bqk=96, ret1=100, ret2=102, ret3=104, ret4=106,
            ret5=110, ret6=114, qi1_done=114, qi1=119,
            score0=122, score1=122, score2=124, score3=126, score4=128, score5=130, score6=132, score7=134,
            q0=139, select=140, k0_done=144, k0=150, att0=154, pt0=157, pt1=159, pv0=160, pv1=163, q1=168, k1_done=176,
            k1=183, att2=186, pt2=189, pt3=192, pv2=194, pv3=196, att_end=200,
            res0=204, res1=208, turn0=212, turn1=220, res2=224, turn2=236, out_end=240)
MIX_BLOCKS = UPTO["out_end"] // KB

VEC = {}
for _name, _n in (("mu_r", 4), ("mu_k", 4), ("mu_v", 4), ("mu_wl", 1), ("mu_al", 1), ("mu_gl", 2),
                  ("w0", 4), ("a0", 4), ("v0", 4), ("k_k", 4), ("k_a", 4), ("r_k", 4)):
    VEC[_name] = (sum(n for _, n in VEC.values()), _n)
N_VEC = sum(n for _, n in VEC.values())

CONST = {}
for _name, _n in (("ident", P), ("rope", NT * 2 * (A_HALF + I_HALF + R_HALF)), ("headmask", 4 * 8),
                  ("gram_mask", 4 * CH), ("level_mask", 6 * CH), ("ident64", CH)):
    CONST[_name] = (sum(n for _, n in CONST.values()), _n)
N_CONST = sum(n for _, n in CONST.values())
ROPE_AT = {"A": (0, A_HALF), "I": (2 * A_HALF, I_HALF), "R": (2 * (A_HALF + I_HALF), R_HALF)}


class Flag:

    def __init__(self, sem, per):
        self.sem, self.per = sem, per

    def at(self, layer, k=0):
        return layer * self.per + k + 1


def build(nc, x_in, stream, consts, decay_in, headmask_t, vecs, wlb, alb, vlb, glb, lnx, gain_cols, final_gain, out,
          v_keep, x_keep):
    base = (nc.sbuf_base + 63) // 64 * 64
    KIB = 1024
    MIX = base + 120 * KIB

    def place(name, shape, offset, dt=F32):
        return nc.alloc_sbuf_tensor_at(name, shape, dt, offset=offset)

    def mix(name, shape, kib, dt=F32):
        return place(name, shape, MIX + int(kib * KIB), dt)

    with ExitStack() as ctx:
        ps = ctx.enter_context(nc.psum_tensor("ps", [P, 8, 512], F32))

        def flag(name, per):
            return Flag(ctx.enter_context(nc.semaphore(name)), per)

        def sem(name):
            return ctx.enter_context(nc.semaphore(name))

        x = place("x", [P, NT, D], base)
        act_hi = place("act_hi", [P, NT, KT, P], base + 16 * KIB, F32R)
        act_lo = place("act_lo", [P, NT, KT, P], base + 32 * KIB, F32R)
        raw = place("raw", [P, 4, BLK], base + 48 * KIB)
        w_hi = place("w_hi", [P, 2, BLK], base + 80 * KIB, F32R)
        w_lo = place("w_lo", [P, 2, BLK], base + 96 * KIB, F32R)
        cst = place("cst", [P, N_CONST], base + 112 * KIB)
        small_at = [base + 112 * KIB + -(-4 * N_CONST // 32) * 32]

        def small(name, shape):
            t = place(name, shape, small_at[0])
            small_at[0] += -(-4 * int(np.prod(shape[1:])) // 32) * 32
            assert small_at[0] <= MIX
            return t

        vec = small("vec", [P, DEPTH, N_VEC])
        gains = small("gains", [P, 2 * DEPTH * KT])
        inv8 = small("inv8", [8, SEQ])
        chunk_decay = small("chunk_decay", [P, 16])
        bonus = small("bonus", [P, 16])
        wi = small("wi", [P, NT, I_HEADS])
        top8 = small("top8", [P, 8])
        gsum = small("gsum", [P, 16])
        gvar = small("gvar", [P, 16])
        nmax = small("nmax", [P, 8])
        rsum = small("rsum", [P, 8])
        sq_parts = small("sq_parts", [P, NT, 4])
        rstd = small("rstd", [P, NT])

        ff_hi = place("ff_hi", [P, NT, FK, P], MIX, F32R)
        ff_lo = place("ff_lo", [P, NT, FK, P], MIX + 44 * KIB, F32R)
        junk = [mix("junk_down", [P, NT, TW], 88), mix("junk_out", [P, NT, TW], 60)]
        gain_row = place("gain_row", [P, D], base + 16 * KIB)
        cat_h = [mix(f"cat_hi{q}", [P, NT, KB, P], k, F32R) for q, k in enumerate((0, 8, 68, 73))]
        cat_l = [mix(f"cat_lo{q}", [P, NT, KB, P], k, F32R) for q, k in enumerate((4, 12, 44, 77))]
        ff_act = mix("ff_act", [P, NT, TW], 88)
        rT = mix("rT", [P, 4, SEQ], 0)
        kT_c = mix("kT_c", [P, 4, SEQ], 4)
        vT_c = mix("vT_c", [P, 4, SEQ], 8)
        tailT = mix("tailT", [P, 4, SEQ], 12)
        narrowT = mix("narrowT", [NARROW, SEQ], 16)
        shift = mix("shift", [P, 4, SEQ], 17)
        g_tok = mix("g_tok", [P, NT, C_W], 17)
        wlb_sb = mix("wlb_sb", [DECAY_LORA, C_W], 21)
        alb_sb = mix("alb_sb", [AAA_LORA, C_W], 23)
        v_tok_c = mix("v_tok_c", [P, NT, C_W], 21)
        vlb_sb = mix("vlb_sb", [P, 2, C_W], 84)
        glb_sb = mix("glb_sb", [P, 2, C_W], 27)
        out_add = mix("out_add", [P, NT, C_W], 27)
        lnx_sb = mix("lnx_sb", [P, 2, C_W], 31)
        hmt_sb = mix("hmt_sb", [8, C_W], 35)
        Pd = mix("Pd", [P, 4, SEQ], 37)
        w_c = mix("w_c", [P, 4, SEQ], 41)
        a_c = mix("a_c", [P, 4, SEQ], 45)
        kk = mix("kk", [P, 4, SEQ], 49)
        kh = mix("kh", [P, 4, SEQ], 53)
        AR = mix("AR", [P, 16, 2, CH], 57)
        starts = mix("starts", [P, 4 * SEQ], 61)
        BT = mix("BT", [P, 4, SEQ], 65)
        KTl = mix("KTl", [P, 4, SEQ], 69)
        b_tok = mix("b_tok", [P, NT, C_W], 73)
        k_tok = mix("k_tok", [P, NT, C_W], 77)
        G = mix("G", [P, NT, 8, 4, CH], 0)
        Tm = mix("Tm", [P, NT, 8, CH], 41)
        Tt = mix("Tt", [P, NT, 4, 2, CH], 45)
        Xm = mix("Xm", [P, NT, 2, 4, CH], 49)
        Mk = mix("Mk", [P, NT, 8, CH], 53)
        y_c = mix("y_c", [P, NT, C_W], 37)
        S = mix("S", [P, 4, CH], 65)
        S_tmp = mix("S_tmp", [P, 4, CH], 66)
        S_bd = mix("S_bd", [P, 4, 2, CH], 67)
        W_sb = mix("W_sb", [P, C_W], 69)
        av = mix("av", [P, NT, C_W], 49)
        U_sb = mix("U_sb", [P, C_W], 71)
        yc_c = mix("yc_c", [P, NT, C_W], 41)
        sq_c = mix("sq_c", [P, NT, C_W], 49)
        tok_c = [mix("tok_c0", [P, NT, TW], 73), mix("tok_c1", [P, NT, TW], 77)]
        tok_a = [mix("tok_a0", [P, NT, TW], 84), mix("tok_a1", [P, NT, TW], 88)]
        rope_tmp = mix("rope_tmp", [P, 4, 512], 8)
        qiT = mix("qiT", [P, 8, SEQ], 16)
        kiT = mix("kiT", [P, SEQ], 92)
        ki2 = mix("ki2", [P, NT, 2, I_DIM], 83)
        qT = mix("qT", [P, 8, SEQ], 28)
        kT = mix("kT", [P, 8, SEQ], 36)
        work = mix("work", [P, NT, SEQ], 81)
        relu = mix("relu", [P, 2, 2, 2, SEQ], 60)
        keep = mix("keep", [P, NT, SEQ], 93)
        Sx = [mix("Sx0", [P, 4, SEQ], 48), mix("Sx1", [P, 4, SEQ], 52)]
        PT = [mix("PT0", [P, 4, 2, P], 56), mix("PT1", [P, 4, 2, P], 60)]
        bT = mix("bT", [P, 4, SEQ], 24)
        decay = mix("decay", [P, 4, 384], 44)
        SB = mix("SB", [P, 4, 384], 50)
        y_b = mix("y_b", [P, NT, TW], 56)
        yc_b = mix("yc_b", [P, NT, TW], 0)
        sq_b = mix("sq_b", [P, NT, TW], 4)
        x_cols = [x[:, :, q * TW:(q + 1) * TW] for q in range(4)]
        v_tok = (x_cols[0], x_cols[3])
        bv, bg = x_cols[1], x_cols[2]
        tok_n = mix("tok_n", [P, NT, NARROW], 81)

        def const(name):
            at, n = CONST[name]
            return cst[:, at:at + n]

        ident = const("ident")
        headmask = const("headmask").rearrange("p (b h) -> p b h", b=4)
        gram_mask = const("gram_mask")
        level_mask = const("level_mask").rearrange("p (l c) -> p l c", l=6)
        ident64 = const("ident64")
        rope_tab = const("rope").rearrange("p (t c) -> p t c", t=NT)

        def vcol(layer, name, k=0):
            at = VEC[name][0] + k
            return vec[:, layer, at:at + 1]

        def gain_col(m, k):
            return gains[:, m * KT + k:m * KT + k + 1]

        def vbc(layer, name):
            at = VEC[name][0]
            return vec[:, layer, at:at + 4].unsqueeze(2).to_broadcast([P, 4, SEQ])

        def over_mid(ap, n):
            return ap.unsqueeze(1).to_broadcast([ap.shape[0], n, ap.shape[1]])

        def last(ap, n):
            return ap.unsqueeze(2).to_broadcast([ap.shape[0], ap.shape[1], n])

        def flat(ap):
            names = "abcd"[:len(ap.shape) - 1]
            return ap.rearrange(f"p {' '.join(names)} -> p ({' '.join(names)})")

        def bank(b, w=512):
            return ps[:, b, 0:w]

        def banks(b, n):
            return ps[:, b:b + n, :]

        x_loaded = [sem(f"x_loaded{q}") for q in range(4)]
        ident_loaded, gains_loaded, consts_loaded = sem("ident_loaded"), sem("gains_loaded"), sem("consts_loaded")
        raw_loaded = [sem(f"raw_loaded{s}") for s in range(4)]
        hi_ready, lo_ready, mm_done = sem("hi_ready"), sem("lo_ready"), sem("mm_done")
        act_chain, dve_chain = sem("act_chain"), sem("dve_chain")

        gain_loaded = sem("gain_loaded")
        sq_summed, var_ready = sem("sq_summed"), sem("var_ready")
        std_ready, rstd_ready = sem("std_ready"), sem("rstd_ready")
        x_turned = sem("x_turned")
        act_hi_ready, act_lo_ready = sem("act_hi_ready"), sem("act_lo_ready")

        tile_tok = flag("tile_tok", N_TILES)
        tile_rot = flag("tile_rot", len(ROTATED))
        tile_turned = flag("tile_turned", len(TURNED))
        tile_ch = flag("tile_ch", len(TURNED))

        c_params = sem("c_params")
        narrow_turned, narrow_tok = flag("narrow_turned", 1), flag("narrow_tok", 1)
        shifted = flag("shifted", 4)
        lora_in = flag("lora_in", 1)
        zw_ps, za_ps, zv_ps, g_ps = flag("zw_ps", 1), flag("za_ps", 1), flag("zv_ps", 1), flag("g_ps", 1)
        a_ready, w_ready, sv_ready, g_ready = (flag("a_ready", 1), flag("w_ready", 1),
                                               flag("sv_ready", 1), flag("g_ready", 1))
        v_kept, v_first_loaded, v_mixed = flag("v_kept", 16), flag("v_first_loaded", 1), flag("v_mixed", 1)
        sqk_ready, ss_ps, nrm_ready, inv_ready, invb_ps = (flag("sqk_ready", 1), flag("ss_ps", 1),
                                                           flag("nrm_ready", 1), flag("inv_ready", 1),
                                                           flag("invb_ps", 1))
        ark_ready, rkk_ready = flag("ark_ready", 1), flag("rkk_ready", 1)
        turned_c, tok_ready, bonus_ps, bonus_ready = (flag("turned_c", 3), flag("tok_ready", 3),
                                                      flag("bonus_ps", 1), flag("bonus_ready", 1))
        gram_ps, gram_ready = flag("gram_ps", 4), flag("gram_ready", 4)
        mk_ready, x_ps, x_ready = flag("mk_ready", 12), flag("x_ps", 12), flag("x_ready", 8)
        ix_ready, t_ps, t_ready = flag("ix_ready", 2), flag("t_ps", 10), flag("t_ready", 12)
        t_turned, tt_ready = flag("t_turned", 10), flag("tt_ready", 10)
        s_zeroed = flag("s_zeroed", 1)
        pre_ps, pre_ready = flag("pre_ps", 1), flag("pre_ready", 1)
        w_ps, w_sbr, u_ps, u_sbr = flag("w_ps", 3), flag("w_sbr", 3), flag("u_ps", 4), flag("u_sbr", 4)
        y_ps, y_sbr, s_ps, s_sbr = flag("y_ps", 4), flag("y_sbr", 4), flag("s_ps", 3), flag("s_sbr", 3)
        gvar_ready, gstd_ready = flag("gvar_ready", 2), flag("gstd_ready", 2)
        oc_ready, oc_turned = flag("oc_ready", 1), flag("oc_turned", 1)

        x_kept, x_back = sem("x_kept"), [sem(f"x_back{q}") for q in range(4)]
        score_ps, relu_ready, relu_used = flag("score_ps", 8), flag("relu_ready", 8), flag("relu_used", 8)
        topk_done = flag("topk_done", 1)
        att_ps, masked, exp_ready, p_ready = (flag("att_ps", 4), flag("masked", 4), flag("exp_ready", 4),
                                              flag("p_ready", 4))
        p_turned, pT_ready, pv_ps = flag("p_turned", 4), flag("pT_ready", 4), flag("pv_ps", 4)
        decay_loaded = sem("decay_loaded")
        bs_ps, sb_ready, yb_ps, yb_ready = flag("bs_ps", 1), flag("sb_ready", 1), flag("yb_ps", 1), flag("yb_ready", 1)
        ob_ready, ob_turned = flag("ob_ready", 1), flag("ob_turned", 1)
        cat_hi, cat_lo = flag("cat_hi", 6), flag("cat_lo", 6)
        resid_out, resid_down = flag("resid_out", 4), flag("resid_down", 4)
        silu_ready, ffa_ready, ffa_turned = flag("silu_ready", FT), flag("ffa_ready", FT), flag("ffa_turned", FT)
        ff_hi_ready, ff_lo_ready = flag("ff_hi_ready", FT), flag("ff_lo_ready", FT)
        out_ready, stored = sem("out_ready"), sem("stored")

        block = ctx.enter_context(nc.Block())

        @block.sync
        def _(sp):
            sp.dma_start(ident, consts[:, 0:P]).then_inc(ident_loaded, 16)
            sp.dma_start(gains[:, :], gain_cols).then_inc(gains_loaded, 16)
            for q in range(4):
                cols = slice(q * TW, (q + 1) * TW)
                sp.dma_start(x[:, :, cols], x_in[:, cols].rearrange("(t p) n -> p t n", p=P))\
                  .then_inc(x_loaded[q], 16)
                sp.dma_start(raw[:, q, :], stream[q * P:(q + 1) * P, :]).then_inc(raw_loaded[q], 16)
            with sp.Fori(1, N_BLOCKS // 4) as i:
                for s in range(4):
                    sp.wait_ge(lo_ready, i * 4 + (s - 3))
                    sp.dma_start(raw[:, s, :], stream[bass.ds(i * (4 * P) + s * P, P), :])\
                      .then_inc(raw_loaded[s], 16)
            for k in range(2 * NT):
                t, cols = k // 2, slice((k % 2) * (D // 2), (k % 2 + 1) * (D // 2))
                sp.wait_ge(out_ready, k + 1)
                sp.dma_start(out[t * P:(t + 1) * P, cols], x[:, t, cols]).then_inc(stored, 16)
            sp.wait_ge(stored, 32 * NT)

        @block.gpsimd
        def _(pool):
            pool.wait_ge(raw_loaded[1], 16)
            pool.dma_start(cst[:, P:], consts[:, P:]).then_inc(consts_loaded, 16)
            pool.dma_start(flat(vec[:, :, :]), vecs).then_inc(consts_loaded, 16)
            for l in range(DEPTH):
                if l > 0:
                    pool.wait_ge(mm_done, LAYER_BLOCKS * l)
                pool.dma_start(wlb_sb[:, :], wlb[l]).then_inc(c_params, 16)
                pool.dma_start(alb_sb[:, :], alb[l]).then_inc(c_params, 16)
                pool.dma_start(vlb_sb[:, :, :], vlb.rearrange("(k p) n -> p k n", p=P)).then_inc(c_params, 16)
                pool.dma_start(glb_sb[:, :, :], glb[l].rearrange("(k p) n -> p k n", p=P)).then_inc(c_params, 16)
                pool.dma_start(flat(lnx_sb[:, :, :]), lnx[l:l + 1, :].partition_broadcast(P)
                               .rearrange("p a d -> p (a d)")).then_inc(c_params, 16)
                pool.dma_start(hmt_sb[:, :], headmask_t).then_inc(c_params, 16)
                if l == 0:
                    pool.wait_ge(shifted.sem, shifted.at(l, T_V))
                    pool.dma_start(v_keep, flat(vT_c[:, :, :])).then_inc(v_kept.sem, 16)
                else:
                    pool.wait_ge(v_kept.sem, 16)
                    pool.dma_start(flat(BT[:, :, :]), v_keep).then_inc(v_first_loaded.sem, 16)
                pool.wait_ge(oc_turned.sem, oc_turned.at(l))
                pool.dma_start(flat(decay[:, :, :]), decay_in).then_inc(decay_loaded, 16)

                def back(q):
                    cols = slice(q * TW, (q + 1) * TW)
                    pool.dma_start(x_cols[q], (x_in if l == 0 else x_keep)[:, cols]
                                   .rearrange("(t p) n -> p t n", p=P)).then_inc(x_back[q], 16)

                pool.wait_ge(ob_ready.sem, ob_ready.at(l))
                pool.wait_ge(pv_ps.sem, pv_ps.at(l, 1))
                if l > 0:
                    pool.wait_ge(x_kept, 16 * 4 * l)
                back(0)
                back(1)
                back(2)
                pool.wait_ge(pv_ps.sem, pv_ps.at(l, 3))
                back(3)
                if l < DEPTH - 1:
                    for q in range(4):
                        cols = slice(q * TW, (q + 1) * TW)
                        pool.wait_ge(resid_down.sem, resid_down.at(l, q))
                        pool.dma_start(x_keep[:, cols].rearrange("(t p) n -> p t n", p=P), x_cols[q])\
                            .then_inc(x_kept, 16)
            pool.wait_ge(mm_done, LAYER_BLOCKS * (DEPTH - 1) + DOWN_B0)
            pool.dma_start(gain_row[:, :], final_gain.partition_broadcast(P).rearrange("p a d -> p (a d)"))\
                .then_inc(gain_loaded, 16)

        @block.scalar
        def _(act):
            links = [0]

            def link(ins):
                links[0] += 1
                ins.then_inc(act_chain, 1)
                act.wait_ge(act_chain, links[0])

            def copy(o, i):
                return act.activation(o, i, ACT.Copy)

            def hi_block(n, w=BLK):
                act.wait_ge(raw_loaded[n % 4], (n // 4 + 1) * 16)
                if n >= 2:
                    act.wait_ge(mm_done, n - 1)
                copy(w_hi[:, n % 2, 0:w], raw[:, n % 4, 0:w]).then_inc(hi_ready, 1)

            def x_done(m, q):
                if m == 0:
                    act.wait_ge(x_loaded[q], 16)
                else:
                    r = resid_down if m % 2 == 0 else resid_out
                    act.wait_ge(r.sem, r.at((m - 1) // 2, q))

            def square(m, q):
                x_done(m, q)
                for t in range(NT):
                    act.activation(junk[m % 2][:, t, :], x[:, t, q * TW:(q + 1) * TW], ACT.Square,
                                   accum_out=sq_parts[:, t, q:q + 1]).then_inc(sq_summed, 1)
                act.wait_ge(sq_summed, NT * (4 * m + q + 1))

            def norm_hi(m, q):
                act.wait_ge(x_turned, 4 * m + q + 1)
                if m > 0:
                    act.wait_ge(mm_done, (m - 1) // 2 * LAYER_BLOCKS + (DOWN_B0 if m % 2 == 0 else OUT_B0))
                for c in range(KB):
                    e = act.activation(act_hi[:, :, KB * q + c, :],
                                       banks(4 + 2 * (q % 2), 2)[:, :, c * P:(c + 1) * P], ACT.Copy,
                                       scale=gain_col(m, KB * q + c))
                e.then_inc(act_hi_ready, 1)

            def std(m):
                act.wait_ge(var_ready, m + 1)
                act.activation(rstd[:, :], rstd[:, :], ACT.Sqrt).then_inc(std_ready, 1)

            def start(m, n):
                hi_block(n)
                hi_block(n + 1)
                square(m, 3)
                hi_block(n + 2)
                norm_hi(m, 3)
                std(m)
                hi_block(n + 3)

            def scaled(dst, b0, w=TW, func=ACT.Copy):
                for t in range(NT):
                    e = act.activation(dst[:, t, :], bank(b0 + t, w), func, scale=rstd[:, t:t + 1])
                return e

            act.wait_ge(gains_loaded, 16)
            norm_hi(0, 0)
            hi_block(0)
            norm_hi(0, 1)
            hi_block(1)
            norm_hi(0, 2)
            square(0, 0)
            hi_block(2)
            norm_hi(0, 3)
            square(0, 1)
            hi_block(3)
            square(0, 2)
            square(0, 3)
            std(0)
            for l in range(DEPTH):
                nb = l * LAYER_BLOCKS

                def tile_hi(j):
                    for b in range(first_block(j), first_block(j + 1)):
                        hi_block(nb + b, NARROW_KB * NARROW if j == T_NARROW else BLK)

                made = [0]
                m0 = nb + first_block(T_V0)

                def hi(point):
                    while made[0] < min(UPTO[point] // KB + 2, MIX_BLOCKS):
                        b = made[0]
                        hi_block(m0 + b)
                        made[0] += 1
                        if b % KB == 1 and T_V0 <= T_V0 + b // KB - 1 < N_TILES:
                            evacuate(T_V0 + b // KB - 1)

                def evacuate(j):
                    if j == T_V0 and l > 0:
                        act.wait_ge(x_kept, 16 * 4 * l)
                    if j in (T_V0, T_V1, T_BV):
                        to_tok(j, {T_V0: v_tok[0], T_V1: v_tok[1], T_BV: bv}[j])
                    elif j == T_BG:
                        scaled(bg, acc(j), func=ACT.Silu).then_inc(tile_tok.sem, 1)
                    else:
                        before = {T_QI1: T_BQK, T_Q0: T_QI0, T_K0: T_QI1, T_Q1: T_Q0, T_K1: T_K0}
                        to_tok(j, tok_a[j % 2], before.get(j))

                def acc(j):
                    act.wait_ge(mm_done, nb + first_block(j + 1))
                    return 2 * (j % 2)

                def to_tok(j, dst, before=None):
                    if before is not None:
                        act.wait_ge(tile_turned.sem, tile_turned.at(l, TURNED.index(before)))
                    scaled(dst, acc(j)).then_inc(tile_tok.sem, 1)

                if l > 0:
                    start(2 * l, nb)
                hi_block(nb + 4)
                hi_block(nb + 5)
                act.wait_ge(rstd_ready, 2 * l + 1)
                to_tok(T_R, tok_c[0][:, :, :])
                hi_block(nb + 6)
                hi_block(nb + 7)
                hi_block(nb + 8)
                hi_block(nb + 9)
                to_tok(T_K, tok_c[1][:, :, :])
                hi_block(nb + 10)
                hi_block(nb + 11)
                hi_block(nb + 12)
                hi_block(nb + 13)
                to_tok(T_V, tok_c[0][:, :, :], T_R)
                hi_block(nb + 14)
                hi_block(nb + 15)
                tile_hi(T_NARROW)
                to_tok(T_TAIL, tok_c[1][:, :, :], T_K)
                hi("start")
                act.wait_ge(mm_done, nb + first_block(T_NARROW + 1))
                copy(narrowT[:, :], ps[0:NARROW, 0, 0:SEQ]).then_inc(tile_tok.sem, 1)
                hi("keys0")
                act.wait_ge(narrow_turned.sem, narrow_turned.at(l))
                for t in range(NT):
                    e = act.activation(tok_n[:, t, :], ps[:, 4, t * NARROW:(t + 1) * NARROW], ACT.Copy,
                                       scale=rstd[:, t:t + 1])
                e.then_inc(narrow_tok.sem, 1)

                act.wait_ge(shifted.sem, shifted.at(l, 3))
                act.activation(tailT[0:DECAY_LORA, 0, :], tailT[0:DECAY_LORA, 0, :], ACT.Tanh)
                act.activation(tailT[:, 2:4, :], tailT[:, 2:4, :], ACT.Sigmoid).then_inc(lora_in.sem, 1)
                if l == 0:
                    act.wait_ge(consts_loaded, 32)
                hi("keys1")
                act.wait_ge(za_ps.sem, za_ps.at(l))
                for b in range(4):
                    last_a = act.activation(a_c[:, b, :], flat(banks(6, 2))[:, b * SEQ:(b + 1) * SEQ], ACT.Sigmoid,
                                            bias=vcol(l, "a0", b))
                last_a.then_inc(a_ready.sem, 1)
                hi("keys")
                act.wait_ge(zw_ps.sem, zw_ps.at(l))
                for b in range(4):
                    last_w = act.activation(w_c[:, b, :], flat(banks(4, 2))[:, b * SEQ:(b + 1) * SEQ], ACT.Sigmoid,
                                            bias=vcol(l, "w0", b))
                link(last_w)
                act.activation(w_c[:, :, :], w_c[:, :, :], ACT.Exp, scale=-EXP_M_HALF).then_inc(w_ready.sem, 1)
                if l > 0:
                    act.wait_ge(zv_ps.sem, l)
                    for b in range(4):
                        last_v = act.activation(KTl[:, b, :], flat(banks(4, 2))[:, b * SEQ:(b + 1) * SEQ],
                                                ACT.Sigmoid, bias=vcol(l, "v0", b))
                    last_v.then_inc(sv_ready.sem, 1)
                act.wait_ge(g_ps.sem, g_ps.at(l))
                act.wait_ge(tile_rot.sem, tile_rot.at(l, 0))
                copy(g_tok[:, :, :], banks(6, 2)).then_inc(g_ready.sem, 1)
                hi("decay")
                hi("gate")
                act.wait_ge(ss_ps.sem, ss_ps.at(l))
                act.activation(inv8[:, :], ps[0:8, 4, 0:SEQ], ACT.Sqrt).then_inc(nrm_ready.sem, 1)
                hi("norm1")
                hi("rate5")
                for n, (dst, b) in enumerate(((b_tok, 4), (k_tok, 6), (v_tok_c, 4))):
                    act.wait_ge(turned_c.sem, turned_c.at(l, n))
                    copy(dst[:, :, :], banks(b, 2)).then_inc(tok_ready.sem, 1)
                act.wait_ge(bonus_ps.sem, bonus_ps.at(l))
                copy(bonus[:, :], bank(6, 16)).then_inc(bonus_ready.sem, 1)
                hi("turned")
                hi("gram")
                hi("level0")
                for lev in range(6):
                    for t in range(NT):
                        if 0 < lev < 5:
                            act.wait_ge(x_ps.sem, x_ps.at(l, 2 * lev + t))
                            copy(Xm[:, t, :, :, :].rearrange("p c b n -> p c (b n)"),
                                 banks(4 + 2 * t, 2)[:, :, 0:4 * CH]).then_inc(x_ready.sem, 1)
                    if lev < 5:
                        hi(f"turn_t{lev + 1}")
                        for t in range(NT):
                            act.wait_ge(t_turned.sem, t_turned.at(l, 2 * lev + t))
                            copy(flat(Tt[:, t, :, :, :]), bank(4 + 2 * t)).then_inc(tt_ready.sem, 1)
                        hi(f"level{lev + 1}")
                hi("inverse")
                act.wait_ge(pre_ps.sem, pre_ps.at(l))
                copy(av[:, :, :], banks(4, 2))
                copy(y_c[:, :, :], banks(6, 2)).then_inc(pre_ready.sem, 1)
                hi("pre")
                for c in range(NCH):
                    r = slice((c % 2) * CH, (c % 2) * CH + CH)
                    act.wait_ge(u_ps.sem, u_ps.at(l, c))
                    copy(U_sb[r, :], ps[r, 5, :]).then_inc(u_sbr.sem, 1)
                    hi(f"u{c}")

                def group_std(k, n):
                    act.wait_ge(gvar_ready.sem, gvar_ready.at(l, k))
                    act.activation(gvar[:, 0:n], gvar[:, 0:n], ACT.Sqrt).then_inc(gstd_ready.sem, 1)

                hi("out2")
                group_std(0, 16)
                hi("out4")
                act.wait_ge(oc_turned.sem, oc_turned.at(l))
                copy(flat(cat_h[Q_C][:, :, :, :]), flat(banks(4, 2))).then_inc(cat_hi.sem, 1)

                hi("bqk")
                hi("ret1")
                hi("ret2")
                act.wait_ge(yb_ps.sem, yb_ps.at(l))
                copy(y_b[:, :, :], banks(4, 2)).then_inc(yb_ready.sem, 1)
                hi("ret3")
                hi("ret4")
                group_std(1, 8)
                hi("ret6")
                act.wait_ge(ob_turned.sem, ob_turned.at(l))
                copy(flat(cat_h[Q_B][:, :, :, :]), flat(banks(4, 2))).then_inc(cat_hi.sem, 1)
                hi("qi1_done")
                hi("qi1")

                for k in range(8):
                    ns = P * (k // 4 + 1)
                    hi(f"score{k}")
                    act.wait_ge(score_ps.sem, score_ps.at(l, k))
                    if k >= 2:
                        act.wait_ge(relu_used.sem, relu_used.at(l, k - 2))
                    act.activation(relu[:, k % 2, :, :, 0:ns],
                                   banks(4 + 2 * (k % 2), 2).rearrange("p o (a s) -> p o a s", a=2)[:, :, :, 0:ns],
                                   ACT.Relu).then_inc(relu_ready.sem, 1)
                hi("q0")
                hi("select")
                hi("k0_done")
                hi("k0")
                hi("att0")

                def exponentials(u):
                    ns = P * (u % 2 + 1)
                    act.wait_ge(masked.sem, masked.at(l, u))
                    for h in range(4):
                        col = 4 * (u % 2) + h
                        e = act.activation(Sx[u % 2][:, h, 0:ns], Sx[u % 2][:, h, 0:ns], ACT.Exp,
                                           bias=nmax[:, col:col + 1], accum_out=rsum[:, col:col + 1])
                    e.then_inc(exp_ready.sem, 1)

                def take_turned(u):
                    nk = u % 2 + 1
                    act.wait_ge(p_turned.sem, p_turned.at(l, u))
                    copy(flat(PT[u % 2][:, 0:2 * nk, :, :])[:, 0:4 * nk * P], flat(banks(4 + 2 * (u % 2), nk)))\
                        .then_inc(pT_ready.sem, 1)

                def attended(u):
                    act.wait_ge(pv_ps.sem, pv_ps.at(l, u))
                    copy(flat(cat_h[u // 2][:, u % 2, :, :]), bank(4 + 2 * (u % 2))).then_inc(cat_hi.sem, 1)

                exponentials(0)
                exponentials(1)
                hi("pt0")
                take_turned(0)
                hi("pt1")
                take_turned(1)
                hi("pv0")
                attended(0)
                hi("pv1")
                attended(1)
                hi("q1")
                hi("k1_done")
                hi("k1")
                hi("att2")
                exponentials(2)
                exponentials(3)
                hi("pt2")
                take_turned(2)
                hi("pt3")
                take_turned(3)
                hi("pv2")
                attended(2)
                hi("pv3")
                attended(3)
                hi("att_end")

                hi("res0")
                hi("res1")
                square(2 * l + 1, 0)
                hi("turn0")
                norm_hi(2 * l + 1, 0)
                square(2 * l + 1, 1)
                hi("turn1")
                norm_hi(2 * l + 1, 1)
                hi("res2")
                hi("turn2")
                square(2 * l + 1, 2)
                norm_hi(2 * l + 1, 2)
                hi("out_end")

                def ffn(i, first):
                    n0 = nb + FFN_B0 + i * 8
                    g = i * 1 + (l * FT)

                    def hi_at(b):
                        s4 = (nb + FFN_B0 + b) % 4
                        act.wait_ge(raw_loaded[s4], i * 32 + ((nb + FFN_B0 + b) // 4 + 1) * 16)
                        act.wait_ge(mm_done, n0 + (b - 1))
                        copy(w_hi[:, b % 2, :], raw[:, s4, :]).then_inc(hi_ready, 1)

                    if first:
                        start(2 * l + 1, n0)
                        act.wait_ge(rstd_ready, 2 * l + 2)
                    else:
                        for b in range(4):
                            hi_at(b)
                        act.wait_ge(ffa_turned.sem, g)
                        turned_hi(i - 1, g)
                    hi_at(4)
                    hi_at(5)
                    act.wait_ge(mm_done, n0 + 4)
                    scaled(ff_act, 0, func=ACT.Silu).then_inc(silu_ready.sem, 1)
                    hi_at(6)
                    hi_at(7)

                def turned_hi(i, g):
                    for t in range(NT):
                        e = copy(flat(ff_hi[:, t, :, :])[:, bass.ds(i * 512, 512)], bank(4 + t))
                    e.then_inc(ff_hi_ready.sem, 1)

                ffn(0, True)
                with act.Fori(1, FT) as i:
                    ffn(i, False)
                for cb in range(4):
                    for b in range(DOWN_PER):
                        hi_block(nb + DOWN_B0 + DOWN_PER * cb + b)
                        if cb == 0 and b == 1:
                            act.wait_ge(ffa_turned.sem, FT * (l + 1))
                            turned_hi(FT - 1, FT * (l + 1))
                        if cb > 0 and b == 3:
                            square(2 * l + 2, cb - 1)
                        if cb > 0 and b == 4 and l < DEPTH - 1:
                            norm_hi(2 * l + 2, cb - 1)
            square(2 * DEPTH, 3)
            std(2 * DEPTH)

        @block.vector
        def _(dve):
            links = [0]

            def link(ins):
                links[0] += 1
                ins.then_inc(dve_chain, 1)
                dve.wait_ge(dve_chain, links[0])

            tt, ts, stt = dve.tensor_tensor, dve.tensor_scalar, dve.scalar_tensor_tensor

            def lo_part(o, i, h):
                return tt(o, i, h.bitcast(F32), ALU.subtract)

            def lo_block(n, w=BLK):
                dve.wait_ge(hi_ready, n + 1)
                lo_part(w_lo[:, n % 2, 0:w], raw[:, n % 4, 0:w], w_hi[:, n % 2, 0:w]).then_inc(lo_ready, 1)

            def norm_lo(m, q):
                dve.wait_ge(act_hi_ready, 4 * m + q + 1)
                for c in range(KB):
                    k = KB * q + c
                    e = stt(act_lo[:, :, k, :], banks(4 + 2 * (q % 2), 2)[:, :, c * P:(c + 1) * P], gain_col(m, k),
                            act_hi[:, :, k, :].bitcast(F32), ALU.mult, ALU.subtract)
                e.then_inc(act_lo_ready, 1)

            def var(m):
                dve.wait_ge(sq_summed, 4 * NT * (m + 1))
                link(dve.tensor_reduce(rstd[:, :], sq_parts[:, :, :], AX.X, ALU.add))
                ts(rstd[:, :], rstd[:, :], 1.0 / D, EPS, ALU.mult, ALU.add).then_inc(var_ready, 1)

            def invert_std(m):
                dve.wait_ge(std_ready, m + 1)
                dve.reciprocal(rstd[:, :], rstd[:, :]).then_inc(rstd_ready, 1)

            def residual(r, l, cb):
                done = OUT_B0 + OUT_DONE[cb] if r is resid_out else DOWN_B0 + DOWN_PER * (cb + 1)
                dve.wait_ge(mm_done, l * LAYER_BLOCKS + done)
                if r is resid_out:
                    dve.wait_ge(x_back[cb], 16 * (l + 1))
                v = x[:, :, cb * TW:(cb + 1) * TW]
                tt(v, v, banks(2 * (cb % 2), 2), ALU.add).then_inc(r.sem, 1)

            def start(m, n):
                lo_block(n)
                residual(resid_down if m % 2 == 0 else resid_out, (m - 1) // 2, 3)
                lo_block(n + 1)
                var(m)
                lo_block(n + 2)
                norm_lo(m, 3)
                invert_std(m)
                lo_block(n + 3)

            dve.wait_ge(gains_loaded, 16)
            for q in range(4):
                norm_lo(0, q)
                lo_block(q)
            var(0)
            invert_std(0)

            def rope(X, kind, heads):
                at, half = ROPE_AT[kind]
                cos = rope_tab[:, :, at:at + half].unsqueeze(2).to_broadcast([P, NT, heads, half])
                sin = rope_tab[:, :, at + half:at + 2 * half].unsqueeze(2).to_broadcast([P, NT, heads, half])
                x1, x2 = X[:, :, :, 0:half], X[:, :, :, half:2 * half]
                tmp = [rope_tmp[:, k, 0:NT * heads * half].rearrange("p (t h f) -> p t h f", t=NT, h=heads)
                       for k in range(4)]
                tt(tmp[0], x1, cos, ALU.mult)
                tt(tmp[1], x2, sin, ALU.mult)
                tt(tmp[2], x2, cos, ALU.mult)
                link(tt(tmp[3], x1, sin, ALU.mult))
                tt(x1, tmp[0], tmp[1], ALU.subtract)
                return tt(x2, tmp[2], tmp[3], ALU.add)

            def centre(y, yc, groups):
                w = NT * 512 // groups
                yg, ycg = (flat(z).rearrange("p (g w) -> p g w", g=groups) for z in (y, yc))
                link(dve.tensor_reduce(gsum[:, 0:groups], yg, AX.X, ALU.add))
                link(ts(gsum[:, 0:groups], gsum[:, 0:groups], 1.0 / w, None, ALU.mult))
                link(tt(ycg, yg, last(gsum[:, 0:groups], w), ALU.subtract))

            def variance(yc, sq, groups, eps):
                w = NT * 512 // groups
                ycg, sqg = (flat(z).rearrange("p (g w) -> p g w", g=groups) for z in (yc, sq))
                link(tt(sqg, ycg, ycg, ALU.mult))
                link(dve.tensor_reduce(gvar[:, 0:groups], sqg, AX.X, ALU.add))
                ts(gvar[:, 0:groups], gvar[:, 0:groups], 1.0 / w, eps, ALU.mult, ALU.add).then_inc(gvar_ready.sem, 1)

            def divide_by_std(l, k, yc, groups):
                w = NT * 512 // groups
                ycg = flat(yc).rearrange("p (g w) -> p g w", g=groups)
                dve.wait_ge(gstd_ready.sem, gstd_ready.at(l, k))
                link(dve.reciprocal(gvar[:, 0:groups], gvar[:, 0:groups]))
                link(tt(ycg, ycg, last(gvar[:, 0:groups], w), ALU.mult))

            for l in range(DEPTH):
                nb = l * LAYER_BLOCKS

                def tile_lo(j):
                    for b in range(first_block(j), first_block(j + 1)):
                        lo_block(nb + b, NARROW_KB * NARROW if j == T_NARROW else BLK)

                made = [0]
                m0 = nb + first_block(T_V0)

                def lo(point):
                    while made[0] < min(UPTO[point] // KB + 2, MIX_BLOCKS):
                        lo_block(m0 + made[0])
                        made[0] += 1

                def from_turned(j, dst, src):
                    k = TURNED.index(j)
                    dve.wait_ge(tile_turned.sem, tile_turned.at(l, k))
                    dve.tensor_copy(dst, src).then_inc(tile_ch.sem, 1)
                    dve.wait_ge(tile_ch.sem, tile_ch.at(l, k))

                def token_shift(k, c, names):
                    r, n = c.shape[0], c.shape[1]
                    d = shift[0:r, 0:n, :]
                    tt(d[:, :, 1:SEQ], c[:, :, 0:SEQ - 1], c[:, :, 1:SEQ], ALU.subtract)
                    link(ts(d[:, :, 0:1], c[:, :, 0:1], -1.0, None, ALU.mult))
                    for b, (name, i) in enumerate(names):
                        e = stt(c[:, b, :], d[:, b, :], vcol(l, name, i)[0:r], c[:, b, :], ALU.mult, ALU.add)
                    e.then_inc(shifted.sem, 1)
                    dve.wait_ge(shifted.sem, shifted.at(l, k))

                def turned_view(b):
                    return banks(b, 2).rearrange("p t (c n) -> p t c n", c=4)

                if l > 0:
                    start(2 * l, nb)
                else:
                    dve.wait_ge(consts_loaded, 32)

                tile_lo(T_K)
                for j, dst, name in ((T_R, rT, "mu_r"), (T_K, kT_c, "mu_k"), (T_V, vT_c, "mu_v")):
                    lo_block(nb + first_block(j + 2), NARROW_KB * NARROW if j == T_V else BLK)
                    from_turned(j, dst[:, :, :].rearrange("p c (t n) -> p t c n", t=NT), turned_view(4 + 2 * (j % 2)))
                    token_shift(j, dst[:, :, :], [(name, i) for i in range(4)])
                    for b in range(first_block(j + 2) + 1, first_block(j + 3)):
                        lo_block(nb + b, NARROW_KB * NARROW if j == T_V else BLK)
                lo("start")
                dve.memset(starts[:, :], 0.0)
                from_turned(T_TAIL, tailT[:, :, :].rearrange("p c (t n) -> p t c n", t=NT), turned_view(6))
                token_shift(3, tailT[:, :, :], [("mu_wl", 0), ("mu_al", 0), ("mu_gl", 0), ("mu_gl", 1)])
                lo("keys0")
                dve.wait_ge(narrow_tok.sem, narrow_tok.at(l))
                at, half = ROPE_AT["I"]
                cos, sin = rope_tab[:, :, at:at + half], rope_tab[:, :, at + half:at + 2 * half]
                x1, x2 = tok_n[:, :, 0:half], tok_n[:, :, half:2 * half]
                tmp = [shift[:, k, 0:NT * half].rearrange("p (t f) -> p t f", t=NT) for k in range(4)]
                tt(tmp[0], x1, cos, ALU.mult)
                tt(tmp[1], x2, sin, ALU.mult)
                tt(tmp[2], x2, cos, ALU.mult)
                link(tt(tmp[3], x1, sin, ALU.mult))
                tt(x1, tmp[0], tmp[1], ALU.subtract)
                tt(x2, tmp[2], tmp[3], ALU.add)
                link(ts(wi[:, :, :], tok_n[:, :, I_DIM:I_DIM + I_HEADS], IDX_W_SCALE, None, ALU.mult))
                for d in range(2):
                    e = dve.tensor_copy(ki2[:, :, d, :], tok_n[:, :, 0:I_DIM])
                e.then_inc(tile_rot.sem, 1)
                lo("keys1")
                k = TURNED.index(T_NARROW)
                dve.wait_ge(tile_turned.sem, tile_turned.at(l, k))
                dve.tensor_copy(kiT[:, :], bank(4, SEQ)).then_inc(tile_ch.sem, 1)
                lo("keys")
                dve.wait_ge(tile_ch.sem, tile_ch.at(l, k))

                link(tt(kk[:, :, :], kT_c[:, :, :], vbc(l, "k_k"), ALU.mult))
                tt(kh[:, :, :], kk[:, :, :], kk[:, :, :], ALU.mult).then_inc(sqk_ready.sem, 1)
                lo("gate")
                dve.wait_ge(w_ready.sem, w_ready.at(l))
                chunk_start = w_c[:, :, :].rearrange("p b (c n) -> p (b c) n", n=CH)[:, :, 0:1]
                link(dve.tensor_copy(starts[:, :].rearrange("p (g n) -> p g n", n=CH)[:, :, 0:1], chunk_start))
                link(dve.memset(chunk_start, 0.0))
                link(dve.tensor_tensor_scan(flat(Pd[:, :, :]), flat(w_c[:, :, :]), starts[:, :], 0.0,
                                            ALU.mult, ALU.add))
                dve.wait_ge(nrm_ready.sem, nrm_ready.at(l))
                link(ts(inv8[:, :], inv8[:, :], KK_EPS, None, ALU.max))
                dve.reciprocal(inv8[:, :], inv8[:, :]).then_inc(inv_ready.sem, 1)
                lo("norm1")
                if l > 0:
                    dve.wait_ge(v_first_loaded.sem, 16 * l)
                    dve.wait_ge(sv_ready.sem, l)
                    link(tt(BT[:, :, :], BT[:, :, :], vT_c[:, :, :], ALU.subtract))
                    link(tt(BT[:, :, :], BT[:, :, :], KTl[:, :, :], ALU.mult))
                    tt(vT_c[:, :, :], vT_c[:, :, :], BT[:, :, :], ALU.add).then_inc(v_mixed.sem, 1)
                    dve.wait_ge(v_mixed.sem, l)
                dve.reciprocal(w_c[:, 0:2, :], Pd[:, 0:2, :])
                lo("rate1")
                dve.reciprocal(w_c[:, 2:4, :], Pd[:, 2:4, :])
                dve.wait_ge(a_ready.sem, a_ready.at(l))
                dve.wait_ge(ss_ps.sem, ss_ps.at(l))
                link(stt(kh[:, :, :], a_c[:, :, :], -1.0, vbc(l, "k_a"), ALU.add, ALU.mult))
                lo("rate2")
                link(stt(kh[:, :, :], kh[:, :, :], 1.0, kT_c[:, :, :], ALU.add, ALU.mult))
                Pg = Pd[:, :, :].rearrange("p b (c n) -> p (b c) n", n=CH)
                dve.tensor_copy(chunk_decay[:, :].unsqueeze(2), Pg[:, :, CH - 1:CH])
                tt(KTl[:, :, :], kh[:, :, :], w_c[:, :, :], ALU.mult)
                rg = rT[:, :, :].rearrange("p b (c n) -> p (b c) n", n=CH)
                link(tt(AR[:, :, 1, :], rg, Pg, ALU.mult))
                lo("rate3")
                dve.wait_ge(invb_ps.sem, invb_ps.at(l))
                link(tt(kk[:, :, :], kk[:, :, :], banks(6, 2).rearrange("p t (b n) -> p (t b) n", b=2), ALU.mult))
                kg = kk[:, :, :].rearrange("p b (c n) -> p (b c) n", n=CH)
                stt(AR[:, :, 0, 1:CH], kg[:, :, 1:CH], -1.0, Pg[:, :, 0:CH - 1], ALU.mult, ALU.mult)
                ts(AR[:, :, 0, 0:1], kg[:, :, 0:1], -1.0, None, ALU.mult)
                link(tt(BT[:, :, :], kk[:, :, :], a_c[:, :, :], ALU.mult))
                lo("rate4")
                tt(BT[:, :, :], BT[:, :, :], w_c[:, :, :], ALU.mult).then_inc(ark_ready.sem, 1)
                for b in range(4):
                    e = stt(kh[:, b, :], kh[:, b, :], vcol(l, "r_k", b), rT[:, b, :], ALU.mult, ALU.mult)
                e.then_inc(rkk_ready.sem, 1)
                lo("rate5")

                lo("turned")
                dve.wait_ge(turned_c.sem, turned_c.at(l, 2))
                if l == 0:
                    dve.wait_ge(v_kept.sem, 16)
                for q in range(4):
                    t, h0 = q // 2, 4 * (q % 2)
                    if q == 2:
                        lo("gram")
                    dve.wait_ge(gram_ps.sem, gram_ps.at(l, q))
                    tt(G[:, t, h0:h0 + 4, :, :].rearrange("p (b o) k n -> p b o (k n)", o=2),
                       banks(4 + 2 * (q % 2), 2).rearrange("p o (b n) -> p b o n", b=2),
                       gram_mask.unsqueeze(1).unsqueeze(1).to_broadcast([P, 2, 2, 4 * CH]), ALU.mult)\
                        .then_inc(gram_ready.sem, 1)

                def level_blocks(lev, t):
                    tt(Mk[:, t, :, :], G[:, t, :, 0, :], over_mid(level_mask[:, lev, :], 8), ALU.mult)\
                        .then_inc(mk_ready.sem, 1)

                def heads_of(b):
                    return bank(b).rearrange("p (h n) -> p h n", h=8)

                def by_head(t):
                    return banks(4 + 2 * t, 2)[:, :, 0:4 * CH].rearrange("p o (b n) -> p b o n", b=4)

                def t_by_head(t):
                    return Tm[:, t, :, :].rearrange("p (b o) n -> p b o n", o=2)

                for t in range(NT):
                    dve.wait_ge(gram_ready.sem, gram_ready.at(l, 2 * t + 1))
                    level_blocks(0, t)
                lo("level0")
                for t in range(NT):
                    dve.wait_ge(x_ps.sem, x_ps.at(l, t))
                    tt(Tm[:, t, :, :], heads_of(4 + 2 * t), over_mid(ident64, 8), ALU.add).then_inc(t_ready.sem, 1)
                for t in range(NT):
                    level_blocks(1, t)
                for lev in range(1, 6):
                    lo(f"turn_t{lev}")
                    for t in range(NT):
                        dve.wait_ge(x_ps.sem, x_ps.at(l, 2 * lev + t))
                        if lev < 5:
                            level_blocks(lev + 1, t)
                        else:
                            tt(Xm[:, t, :, :, :],
                               banks(4 + 2 * t, 2)[:, :, 0:4 * CH].rearrange("p c (b n) -> p c b n", b=4),
                               ident64.unsqueeze(1).unsqueeze(1).to_broadcast([P, 2, 4, CH]), ALU.add)\
                                .then_inc(ix_ready.sem, 1)
                    for t in range(NT):
                        k = 2 * lev + t
                        dve.wait_ge(t_ready.sem, t_ready.at(l, k - 2))
                        dve.wait_ge(t_ps.sem, t_ps.at(l, k - 2))
                        if lev < 5:
                            tt(t_by_head(t), t_by_head(t), by_head(t), ALU.add).then_inc(t_ready.sem, 1)
                        else:
                            dve.tensor_copy(t_by_head(t), by_head(t)).then_inc(t_ready.sem, 1)
                    lo(f"level{lev}")
                dve.wait_ge(t_ready.sem, t_ready.at(l, 11))
                dve.memset(S[:, :, :], 0.0)
                dve.memset(S_bd[:, :, :, :], 0.0).then_inc(s_zeroed.sem, 1)
                dve.wait_ge(bonus_ready.sem, bonus_ready.at(l))
                dve.wait_ge(g_ready.sem, g_ready.at(l))
                dve.wait_ge(tok_ready.sem, tok_ready.at(l, 2))
                link(tt(out_add[:, :, :].rearrange("p t (h n) -> p (t h) n", h=8),
                        v_tok_c[:, :, :].rearrange("p t (h n) -> p (t h) n", h=8), last(bonus[:, :], W_DIM), ALU.mult))
                link(tt(out_add[:, :, :], out_add[:, :, :], over_mid(lnx_sb[:, 1, :], NT), ALU.add))
                link(tt(out_add[:, :, :], out_add[:, :, :], g_tok[:, :, :], ALU.mult))
                link(tt(g_tok[:, :, :], g_tok[:, :, :], over_mid(lnx_sb[:, 0, :], NT), ALU.mult))
                dve.wait_ge(s_zeroed.sem, s_zeroed.at(l))
                lo("inverse")
                dve.wait_ge(pre_ready.sem, pre_ready.at(l))
                lo("pre")
                cd = chunk_decay[:, :].rearrange("p (b c) -> p b c", b=4)
                for c in range(NCH):
                    t, rc = c // 2, slice((c % 2) * CH, (c % 2) * CH + CH)
                    if c > 0:
                        dve.wait_ge(w_ps.sem, w_ps.at(l, c - 1))
                        tt(W_sb[rc, :], av[rc, t, :], ps[rc, 4, :], ALU.add).then_inc(w_sbr.sem, 1)
                        link(tt(y_c[rc, t, :], y_c[rc, t, :], ps[rc, 6, :], ALU.add))
                    if c < NCH - 1:
                        dve.wait_ge(s_ps.sem, s_ps.at(l, c))
                        link(tt(S_tmp[:, :, :], S[:, :, :], bank(7, 4 * CH).rearrange("p (b n) -> p b n", b=4),
                                ALU.add))
                        for o in range(2):
                            ro = slice(o * CH, o * CH + CH)
                            tt(S_bd[ro, :, o, :], S_tmp[ro, :, :], last(cd[ro, :, c], CH), ALU.mult)
                        tt(S[:, :, :], S_tmp[:, :, :], last(cd[:, :, c], CH), ALU.mult).then_inc(s_sbr.sem, 1)
                        dve.wait_ge(s_sbr.sem, s_sbr.at(l, c))
                    dve.wait_ge(y_ps.sem, y_ps.at(l, c))
                    tt(y_c[rc, t, :], y_c[rc, t, :], ps[rc, 4, :], ALU.add).then_inc(y_sbr.sem, 1)
                    dve.wait_ge(y_sbr.sem, y_sbr.at(l, c))
                    lo(f"u{c}")
                lo("out1")
                centre(y_c[:, :, :], yc_c[:, :, :], 16)
                lo("out2")
                variance(yc_c[:, :, :], sq_c[:, :, :], 16, LNX_EPS)
                divide_by_std(l, 0, yc_c[:, :, :], 16)
                lo("out3")
                link(tt(yc_c[:, :, :], yc_c[:, :, :], g_tok[:, :, :], ALU.mult))
                tt(yc_c[:, :, :], yc_c[:, :, :], out_add[:, :, :], ALU.add).then_inc(oc_ready.sem, 1)

                def rotate(j, tok, kind, heads):
                    dve.wait_ge(tile_tok.sem, tile_tok.at(l, j))
                    rope(tok[:, :, :].rearrange("p t (h n) -> p t h n", h=heads), kind, heads)\
                        .then_inc(tile_rot.sem, 1)

                def gather(j, dst, b):
                    from_turned(j, dst.rearrange("p c (t n) -> p t c n", t=NT), turned_view(b))

                def cat_lo_part(k, dst, src, src_hi):
                    dve.wait_ge(cat_hi.sem, cat_hi.at(l, k))
                    lo_part(flat(dst), src, flat(src_hi)).then_inc(cat_lo.sem, 1)

                def index_scores(k):
                    t = k // 4
                    ns = P * (t + 1)
                    dve.wait_ge(relu_ready.sem, relu_ready.at(l, k))
                    for c in range(4):
                        head = 4 * (k % 4) + c
                        src, wh = relu[:, k % 2, c % 2, c // 2, 0:ns], wi[:, t, head:head + 1]
                        if head == 0:
                            e = ts(work[:, t, 0:ns], src, wh, None, ALU.mult)
                        else:
                            e = stt(work[:, t, 0:ns], src, wh, work[:, t, 0:ns], ALU.mult, ALU.add)
                        if c < 3:
                            link(e)
                        else:
                            e.then_inc(relu_used.sem, 1)
                            dve.wait_ge(relu_used.sem, relu_used.at(l, k))

                def top_k(t, rounds, first=False, final=False):
                    ns = P * (t + 1)
                    w = work[:, t, 0:ns]
                    if first:
                        if t == 0:
                            dve.memset(work[0:CH, 0, CH:2 * CH], INADMISSIBLE)
                        else:
                            dve.memset(work[0:CH, 1, 3 * CH:4 * CH], INADMISSIBLE)
                        link(dve.memset(nmax[:, 0:1], 0.0))
                    for _ in range(rounds):
                        link(dve.max(top8[:, :], w))
                        link(dve.match_replace(w, top8[:, :], w, TAKEN))
                    if final:
                        link(ts(keep[:, t, 0:ns], w, TAKEN, BIG, ALU.is_equal, ALU.mult))
                        e = ts(keep[:, t, 0:ns], keep[:, t, 0:ns], -BIG, None, ALU.add)
                        if t == 1:
                            e.then_inc(topk_done.sem, 1)
                        else:
                            link(e)

                lo("out4")
                rotate(T_BQK, tok_a[T_BQK % 2], "R", 8)
                cat_lo_part(0, cat_l[Q_C][:, :, :, :], flat(banks(4, 2)), cat_h[Q_C][:, :, :, :])
                lo("bqk")
                gather(T_BQK, bT[:, :, :], 6)

                lo("ret1")
                dve.wait_ge(decay_loaded, 16 * (l + 1))
                dve.wait_ge(bs_ps.sem, bs_ps.at(l))
                tt(SB[:, :, :], banks(4, 4)[:, :, 0:384], decay[:, :, :], ALU.mult).then_inc(sb_ready.sem, 1)
                lo("ret2")
                rotate(T_QI0, tok_a[T_QI0 % 2], "I", 8)
                dve.wait_ge(yb_ready.sem, yb_ready.at(l))
                centre(y_b[:, :, :], yc_b[:, :, :], 8)
                lo("ret3")
                gather(T_QI0, qiT[:, 0:4, :], 6)
                lo("ret4")
                variance(yc_b[:, :, :], sq_b[:, :, :], 8, EPS)
                divide_by_std(l, 1, yc_b[:, :, :], 8)
                lo("ret5")
                dve.wait_ge(tile_tok.sem, tile_tok.at(l, T_BG))
                tt(yc_b[:, :, :], yc_b[:, :, :], bg, ALU.mult).then_inc(ob_ready.sem, 1)
                lo("ret6")
                cat_lo_part(1, cat_l[Q_B][:, :, :, :], flat(banks(4, 2)), cat_h[Q_B][:, :, :, :])
                lo("qi1_done")
                rotate(T_QI1, tok_a[T_QI1 % 2], "I", 8)
                lo("qi1")
                gather(T_QI1, qiT[:, 4:8, :], 6)

                for k in range(8):
                    lo(f"score{k}")
                    index_scores(k)
                    if k == 5:
                        rotate(T_Q0, tok_a[T_Q0 % 2], "A", 4)
                lo("q0")
                top_k(0, 5, first=True)
                lo("select")
                top_k(0, 3, final=True)
                gather(T_Q0, qT[:, 0:4, :], 4)
                lo("k0_done")
                top_k(1, 4, first=True)
                rotate(T_K0, tok_a[T_K0 % 2], "A", 4)
                lo("k0")
                top_k(1, 4, final=True)
                gather(T_K0, kT[:, 0:4, :], 6)
                lo("att0")

                def mask(u):
                    t = u % 2
                    ns = P * (t + 1)
                    cols = slice(4 * t, 4 * t + 4)
                    dve.wait_ge(att_ps.sem, att_ps.at(l, u))
                    src = flat(banks(4 + 2 * t, t + 1)).rearrange("p (h s) -> p h s", h=4)
                    link(stt(Sx[t][:, :, 0:ns], src, A_SCALE, over_mid(keep[:, t, 0:ns], 4), ALU.mult, ALU.add))
                    dve.tensor_reduce(nmax[:, cols], Sx[t][:, :, 0:ns], AX.X, ALU.max, negate=True)\
                        .then_inc(masked.sem, 1)

                def divide(u):
                    t = u % 2
                    ns = P * (t + 1)
                    cols = slice(4 * t, 4 * t + 4)
                    dve.wait_ge(exp_ready.sem, exp_ready.at(l, u))
                    link(dve.reciprocal(rsum[:, cols], rsum[:, cols]))
                    tt(Sx[t][:, :, 0:ns], Sx[t][:, :, 0:ns], last(rsum[:, cols], ns), ALU.mult).then_inc(p_ready.sem, 1)

                def attended(u):
                    cat_lo_part(2 + u, cat_l[u // 2][:, u % 2, :, :], bank(4 + 2 * (u % 2)),
                                cat_h[u // 2][:, u % 2, :, :])

                mask(0)
                mask(1)
                divide(0)
                divide(1)
                lo("pt0")
                lo("pt1")
                lo("pv0")
                attended(0)
                rotate(T_Q1, tok_a[T_Q1 % 2], "A", 4)
                lo("pv1")
                attended(1)
                lo("q1")
                gather(T_Q1, qT[:, 4:8, :], 4)
                lo("k1_done")
                rotate(T_K1, tok_a[T_K1 % 2], "A", 4)
                lo("k1")
                gather(T_K1, kT[:, 4:8, :], 6)
                lo("att2")
                mask(2)
                mask(3)
                divide(2)
                divide(3)
                lo("pt2")
                lo("pt3")
                lo("pv2")
                attended(2)
                lo("pv3")
                attended(3)
                lo("att_end")

                lo("res0")
                residual(resid_out, l, 0)
                lo("res1")
                residual(resid_out, l, 1)
                lo("turn0")
                norm_lo(2 * l + 1, 0)
                lo("turn1")
                norm_lo(2 * l + 1, 1)
                lo("res2")
                residual(resid_out, l, 2)
                lo("turn2")
                norm_lo(2 * l + 1, 2)
                lo("out_end")

                def ffn(i, first):
                    n0 = nb + FFN_B0 + i * 8
                    g = i * 1 + (l * FT)

                    def lo_at(b):
                        dve.wait_ge(hi_ready, n0 + (b + 1))
                        lo_part(w_lo[:, b % 2, :], raw[:, (nb + FFN_B0 + b) % 4, :], w_hi[:, b % 2, :])\
                            .then_inc(lo_ready, 1)

                    if first:
                        start(2 * l + 1, n0)
                    else:
                        lo_at(0)
                        lo_at(1)
                        product(n0, g)
                        lo_at(2)
                        lo_at(3)
                        turned_lo(i - 1, g)
                    for b in range(4, 8):
                        lo_at(b)

                def product(done, g):
                    dve.wait_ge(mm_done, done)
                    dve.wait_ge(silu_ready.sem, g)
                    for t in range(NT):
                        e = stt(ff_act[:, t, :], bank(2 + t), rstd[:, t:t + 1], ff_act[:, t, :], ALU.mult, ALU.mult)
                    e.then_inc(ffa_ready.sem, 1)

                def turned_lo(i, g):
                    dve.wait_ge(ff_hi_ready.sem, g)
                    for t in range(NT):
                        e = lo_part(flat(ff_lo[:, t, :, :])[:, bass.ds(i * 512, 512)], bank(4 + t),
                                    flat(ff_hi[:, t, :, :])[:, bass.ds(i * 512, 512)])
                    e.then_inc(ff_lo_ready.sem, 1)

                ffn(0, True)
                with dve.Fori(1, FT) as i:
                    ffn(i, False)

                for cb in range(4):
                    n0 = nb + DOWN_B0 + DOWN_PER * cb
                    for b in range(DOWN_PER):
                        lo_block(n0 + b)
                        if b == 0 and cb == 0:
                            product(nb + DOWN_B0, FT * (l + 1))
                        if b == 1 and cb == 0:
                            turned_lo(FT - 1, FT * (l + 1))
                        if b == 1 and cb > 0:
                            residual(resid_down, l, cb - 1)
                        if b == 4 and cb > 0 and l < DEPTH - 1:
                            norm_lo(2 * l + 2, cb - 1)
            residual(resid_down, DEPTH - 1, 3)
            var(2 * DEPTH)
            invert_std(2 * DEPTH)
            dve.wait_ge(rstd_ready, 2 * DEPTH + 1)
            dve.wait_ge(gain_loaded, 16)
            for k in range(2 * NT):
                t, cols = k // 2, slice((k % 2) * (D // 2), (k % 2 + 1) * (D // 2))
                stt(x[:, t, cols], x[:, t, cols], rstd[:, t:t + 1], gain_row[:, cols], ALU.mult, ALU.mult)\
                    .then_inc(out_ready, 1)

        @block.tensor
        def _(pe):
            mm, turn = pe.matmul, pe.transpose

            def three(acc, st_hi, st_lo, mv_hi, mv_lo, start, stop):
                mm(acc, st_hi, mv_hi, start=start, stop=False)
                mm(acc, st_hi, mv_lo, start=False, stop=False)
                return mm(acc, st_lo, mv_hi, start=False, stop=stop)

            def mm_block(n, s2, hi, lo, k0, nk, w, b0, first, final):
                pe.wait_ge(lo_ready, n)
                for k in range(nk):
                    for t in range(NT):
                        e = three(ps[:, b0 + t, 0:w], hi[:, t, k0 + k, :], lo[:, t, k0 + k, :],
                                  w_hi[:, s2, k * w:(k + 1) * w], w_lo[:, s2, k * w:(k + 1) * w],
                                  first and k == 0, final and k == nk - 1)
                e.then_inc(mm_done, 1)

            def turn_x(m, q):
                if m == 0:
                    pe.wait_ge(x_loaded[q], 16)
                else:
                    r = resid_down if m % 2 == 0 else resid_out
                    pe.wait_ge(r.sem, r.at((m - 1) // 2, q))
                if q >= 2:
                    pe.wait_ge(act_lo_ready, 4 * m + q - 1)
                for t in range(NT):
                    for c in range(KB):
                        k = KB * q + c
                        e = turn(ps[:, 4 + 2 * (q % 2) + t, c * P:(c + 1) * P], x[:, t, k * P:(k + 1) * P], ident)
                e.then_inc(x_turned, 1)

            def x_split(m, q):
                pe.wait_ge(act_lo_ready, 4 * m + q + 1)

            pe.wait_ge(ident_loaded, 16)
            for l in range(DEPTH):
                nb = l * LAYER_BLOCKS

                def tile_blocks(j, b_from, b_to):
                    if b_from == 0:
                        if j >= 2:
                            pe.wait_ge(tile_tok.sem, tile_tok.at(l, j - 2))
                        elif l > 0:
                            pe.wait_ge(resid_down.sem, resid_down.at(l - 1, 2 + j))
                    for b in range(b_from, b_to):
                        n = nb + first_block(j) + b
                        mm_block(n + 1, n % 2, act_hi, act_lo, b * KB, KB, TW, 2 * (j % 2), b == 0, b == KT // KB - 1)

                def tile_mm(j):
                    tile_blocks(j, 0, KT // KB)

                pos = [0]
                cat_at = {Q_C: 0, Q_B: 1, Q_A0: 3, Q_A1: 5}

                def gemm(point):
                    while pos[0] < UPTO[point]:
                        b, k = divmod(pos[0], KB)
                        pos[0] += 1
                        n = nb + first_block(T_V0) + b
                        if n - nb < OUT_B0:
                            j = T_V0 + b // KB
                            hi, lo, b0, kt = act_hi, act_lo, 2 * (j % 2), KB * (b % KB) + k
                            first, final = kt == 0, kt == KT - 1
                            if first:
                                pe.wait_ge(tile_tok.sem, tile_tok.at(l, j - 2))
                        else:
                            cb, q = OUT_ORDER[n - nb - OUT_B0]
                            hi, lo, b0, kt = cat_h[q], cat_l[q], 2 * (cb % 2), k
                            first, final = q == Q_C and k == 0, q == Q_A1 and k == KB - 1
                            if first and cb < 2:
                                pe.wait_ge(tile_tok.sem, tile_tok.at(l, N_TILES - 2 + cb))
                            elif first:
                                pe.wait_ge(resid_out.sem, resid_out.at(l, cb - 2))
                            if k == 0:
                                pe.wait_ge(cat_lo.sem, cat_lo.at(l, cat_at[q]))
                        if k == 0:
                            pe.wait_ge(lo_ready, n + 1)
                        for t in range(NT):
                            e = three(bank(b0 + t), hi[:, t, kt, :], lo[:, t, kt, :],
                                      w_hi[:, n % 2, k * TW:(k + 1) * TW], w_lo[:, n % 2, k * TW:(k + 1) * TW],
                                      first, final)
                        if k == KB - 1:
                            e.then_inc(mm_done, 1)

                def turn_tile(j, src, b):
                    k = TURNED.index(j)
                    if j in ROTATED:
                        pe.wait_ge(tile_rot.sem, tile_rot.at(l, ROTATED.index(j)))
                    else:
                        pe.wait_ge(tile_tok.sem, tile_tok.at(l, j))
                    if k >= 1:
                        pe.wait_ge(tile_ch.sem, tile_ch.at(l, k - 1))
                    for t in range(NT):
                        for c in range(4):
                            e = turn(ps[:, b + t, c * P:(c + 1) * P], src[:, t, c * P:(c + 1) * P], ident)
                    e.then_inc(tile_turned.sem, 1)

                if l == 0:
                    turn_x(0, 0)
                    turn_x(0, 1)
                    for b in range(2):
                        x_split(0, b)
                        turn_x(0, b + 2)
                        tile_blocks(T_R, b, b + 1)
                    x_split(0, 2)
                    tile_blocks(T_R, 2, 3)
                    x_split(0, 3)
                else:
                    x_split(2 * l, 2)
                    tile_blocks(T_R, 0, 1)
                    turn_x(2 * l, 3)
                    tile_blocks(T_R, 1, 3)
                    x_split(2 * l, 3)
                tile_blocks(T_R, 3, 4)
                tile_blocks(T_K, 0, 3)
                turn_tile(T_R, tok_c[0], 4)
                tile_blocks(T_K, 3, 4)
                tile_blocks(T_V, 0, 3)
                turn_tile(T_K, tok_c[1], 6)
                tile_blocks(T_V, 3, 4)
                tile_blocks(T_TAIL, 0, 3)
                turn_tile(T_V, tok_c[0], 4)
                tile_blocks(T_TAIL, 3, 4)
                pe.wait_ge(tile_tok.sem, tile_tok.at(l, T_NARROW - 2))
                for b in range(KT // NARROW_KB):
                    n = nb + first_block(T_NARROW) + b
                    pe.wait_ge(lo_ready, n + 1)
                    for k in range(NARROW_KB):
                        kt = NARROW_KB * b + k
                        cols = slice(k * NARROW, (k + 1) * NARROW)
                        e = three(ps[0:NARROW, 0, 0:SEQ].rearrange("p (t n) -> p t n", t=NT),
                                  w_hi[:, n % 2, cols], w_lo[:, n % 2, cols], act_hi[:, :, kt, :], act_lo[:, :, kt, :],
                                  kt == 0, kt == KT - 1)
                    e.then_inc(mm_done, 1)
                turn_tile(T_TAIL, tok_c[1], 6)
                gemm("keys0")
                pe.wait_ge(tile_tok.sem, tile_tok.at(l, T_NARROW))
                for t in range(NT):
                    e = turn(ps[:, 4, t * NARROW:(t + 1) * NARROW], narrowT[:, t * P:(t + 1) * P],
                             ident[0:NARROW, 0:NARROW])
                e.then_inc(narrow_turned.sem, 1)
                gemm("keys")
                pe.wait_ge(tile_rot.sem, tile_rot.at(l, 0))
                pe.wait_ge(tile_ch.sem, tile_ch.at(l, TURNED.index(T_TAIL)))
                for t in range(NT):
                    e = turn(ps[:, 4, t * P:(t + 1) * P], flat(ki2[:, t, :, :]), ident)
                e.then_inc(tile_turned.sem, 1)

                pe.wait_ge(c_params, 96 * (l + 1))
                pe.wait_ge(lora_in.sem, lora_in.at(l))

                def lora(b0, w_sb, src, rows):
                    for b in range(4):
                        e = mm(flat(banks(b0, 2))[:, b * SEQ:(b + 1) * SEQ], w_sb[0:rows, b * P:(b + 1) * P], src,
                               start=True, stop=True)
                    return e

                lora(6, alb_sb, tailT[0:AAA_LORA, 1, :], AAA_LORA).then_inc(za_ps.sem, 1)
                gemm("decay")
                pe.wait_ge(tile_ch.sem, tile_ch.at(l, TURNED.index(T_NARROW)))
                lora(4, wlb_sb, tailT[0:DECAY_LORA, 0, :], DECAY_LORA).then_inc(zw_ps.sem, 1)
                pe.wait_ge(a_ready.sem, a_ready.at(l))
                for t in range(NT):
                    for k in range(2):
                        e = mm(bank(6 + t), tailT[:, 2 + k, t * P:(t + 1) * P], glb_sb[:, k, :],
                               start=(k == 0), stop=(k == 1))
                e.then_inc(g_ps.sem, 1)
                pe.wait_ge(w_ready.sem, w_ready.at(l))
                if l > 0:
                    for b in range(4):
                        for k in range(2):
                            e = mm(flat(banks(4, 2))[:, b * SEQ:(b + 1) * SEQ], vlb_sb[:, k, b * P:(b + 1) * P],
                                   tailT[:, k, :], start=(k == 0), stop=(k == 1))
                    e.then_inc(zv_ps.sem, 1)
                gemm("gate")
                if l > 0:
                    pe.wait_ge(sv_ready.sem, l)
                if l == 0:
                    pe.wait_ge(consts_loaded, 32)
                pe.wait_ge(sqk_ready.sem, sqk_ready.at(l))
                for b in range(4):
                    e = mm(ps[0:8, 4, 0:SEQ], headmask[:, b, :], kh[:, b, :], start=(b == 0), stop=(b == 3))
                e.then_inc(ss_ps.sem, 1)
                gemm("norm1")
                pe.wait_ge(inv_ready.sem, inv_ready.at(l))
                pe.wait_ge(g_ready.sem, g_ready.at(l))
                for b in range(4):
                    e = mm(flat(banks(6, 2))[:, b * SEQ:(b + 1) * SEQ], hmt_sb[:, b * P:(b + 1) * P], inv8[:, :],
                           start=True, stop=True)
                e.then_inc(invb_ps.sem, 1)
                gemm("rate5")
                pe.wait_ge(ark_ready.sem, ark_ready.at(l))
                for n, (src, b0) in enumerate(((BT, 4), (KTl, 6), (vT_c, 4))):
                    if n == 2:
                        pe.wait_ge(tok_ready.sem, tok_ready.at(l, 0))
                        if l > 0:
                            pe.wait_ge(v_mixed.sem, l)
                    for t in range(NT):
                        for b in range(4):
                            e = turn(ps[:, b0 + t, b * P:(b + 1) * P], src[:, b, t * P:(t + 1) * P], ident)
                    e.then_inc(turned_c.sem, 1)
                pe.wait_ge(rkk_ready.sem, rkk_ready.at(l))
                pe.wait_ge(tok_ready.sem, tok_ready.at(l, 1))
                for t in range(NT):
                    for b in range(4):
                        e = mm(ps[:, 6, 8 * t:8 * t + 8], kh[:, b, t * P:(t + 1) * P], headmask[:, b, :],
                               start=(b == 0), stop=(b == 3))
                e.then_inc(bonus_ps.sem, 1)
                gemm("turned")

                def rows(o):
                    return slice(o * CH, o * CH + CH)

                for q in range(4):
                    t, h0 = q // 2, 4 * (q % 2)
                    if q == 2:
                        gemm("gram")
                    if q == 0:
                        pe.wait_ge(tok_ready.sem, tok_ready.at(l, 2))
                    elif q == 1:
                        pe.wait_ge(bonus_ready.sem, bonus_ready.at(l))
                    else:
                        pe.wait_ge(gram_ready.sem, gram_ready.at(l, q - 2))
                    for h in range(h0, h0 + 4):
                        b, o = h // 2, h % 2
                        for c in range(2):
                            c4 = 2 * t + c
                            bk, col = 4 + 2 * (q % 2) + o, 256 * (b % 2)
                            for src, at in ((BT, 0), (KTl, 128)):
                                e = mm(ps[rows(c), bk, col + at:col + at + 128],
                                       src[rows(o), b, c4 * CH:(c4 + 1) * CH],
                                       AR[rows(o), 4 * b + c4, :, :].rearrange("p k n -> p (k n)"),
                                       start=True, stop=True)
                    e.then_inc(gram_ps.sem, 1)
                for lev in range(6):
                    gemm(f"level{lev}")
                    for t in range(NT):
                        k = 2 * lev + t
                        pe.wait_ge(mk_ready.sem, mk_ready.at(l, k))
                        if lev == 0:
                            pe.wait_ge(gram_ready.sem, gram_ready.at(l, 3))
                        else:
                            pe.wait_ge(tt_ready.sem, tt_ready.at(l, k - 2))
                        for h in range(8):
                            b, o = h // 2, h % 2
                            for c in range(2):
                                if lev == 0:
                                    e = mm(ps[rows(c), 4 + 2 * t, h * CH:(h + 1) * CH], Mk[rows(c), t, h, :],
                                           ident[rows(c), c * CH:(c + 1) * CH], start=True, stop=True)
                                else:
                                    e = mm(ps[rows(o), 4 + 2 * t + c, b * CH:(b + 1) * CH], Mk[rows(c), t, h, :],
                                           Tm[rows(c), t, h, :], start=True, stop=True)
                        e.then_inc(x_ps.sem, 1)
                    if lev > 0:
                        for t in range(NT):
                            if lev < 5:
                                pe.wait_ge(x_ready.sem, x_ready.at(l, 2 * lev + t - 2))
                            else:
                                pe.wait_ge(ix_ready.sem, ix_ready.at(l, t))
                            for h in range(8):
                                b, o = h // 2, h % 2
                                for c in range(2):
                                    dst = ps[rows(c), 4 + 2 * t + o, b * CH:(b + 1) * CH]
                                    tt_h, x_h = Tt[rows(o), t, b, c, :], Xm[rows(o), t, c, b, :]
                                    if lev < 5:
                                        e = mm(dst, tt_h, x_h, start=True, stop=True)
                                    else:
                                        e = mm(dst, x_h, tt_h, start=True, stop=True)
                            e.then_inc(t_ps.sem, 1)
                    if lev < 5:
                        gemm(f"turn_t{lev + 1}")
                        for t in range(NT):
                            pe.wait_ge(t_ready.sem, t_ready.at(l, 2 * lev + t))
                            for b in range(4):
                                e = turn(ps[:, 4 + 2 * t, b * P:(b + 1) * P],
                                         Tm[:, t, 2 * b:2 * b + 2, :].rearrange("p o n -> p (o n)"), ident)
                            e.then_inc(t_turned.sem, 1)
                gemm("inverse")
                pe.wait_ge(t_ready.sem, t_ready.at(l, 11))
                pe.wait_ge(s_zeroed.sem, s_zeroed.at(l))
                for t in range(NT):
                    for h in range(8):
                        for c in range(2):
                            rc, cols = rows(c), slice(h * CH, (h + 1) * CH)
                            mm(ps[rc, 4 + t, cols], G[rc, t, h, 2, :], v_tok_c[rc, t, cols], start=True, stop=True)
                            e = mm(ps[rc, 6 + t, cols], G[rc, t, h, 3, :], v_tok_c[rc, t, cols], start=True, stop=True)
                e.then_inc(pre_ps.sem, 1)
                gemm("pre")
                pe.wait_ge(pre_ready.sem, pre_ready.at(l))
                for c4 in range(NCH):
                    t, c = c4 // 2, c4 % 2
                    rc = rows(c)
                    if c4 > 0:
                        pe.wait_ge(s_sbr.sem, s_sbr.at(l, c4 - 1))
                        for kind, bk in ((0, 4), (1, 6)):
                            for b in range(4):
                                e = mm(ps[rc, bk, b * P:(b + 1) * P], AR[:, 4 * b + c4, kind, :],
                                       S_bd[:, b, :, :].rearrange("p o n -> p (o n)"), start=True, stop=True)
                        e.then_inc(w_ps.sem, 1)
                        gemm(f"w{c4}")
                        pe.wait_ge(w_sbr.sem, w_sbr.at(l, c4 - 1))
                    for h in range(8):
                        cols = slice(h * CH, (h + 1) * CH)
                        src = W_sb[rc, cols] if c4 > 0 else av[rc, t, cols]
                        e = mm(ps[rc, 5, cols], Tm[rc, t, h, :], src, start=True, stop=True)
                    e.then_inc(u_ps.sem, 1)
                    gemm(f"u{c4}")
                    pe.wait_ge(u_sbr.sem, u_sbr.at(l, c4))
                    if c4 < NCH - 1:
                        for h in range(8):
                            b, o, cols = h // 2, h % 2, slice(h * CH, (h + 1) * CH)
                            mm(ps[rows(o), 7, b * CH:(b + 1) * CH], b_tok[rc, t, cols], U_sb[rc, cols],
                               start=True, stop=False)
                            e = mm(ps[rows(o), 7, b * CH:(b + 1) * CH], k_tok[rc, t, cols], v_tok_c[rc, t, cols],
                                   start=False, stop=True)
                        e.then_inc(s_ps.sem, 1)
                    for h in range(8):
                        cols = slice(h * CH, (h + 1) * CH)
                        e = mm(ps[rc, 4, cols], G[rc, t, h, 1, :], U_sb[rc, cols], start=True, stop=True)
                    e.then_inc(y_ps.sem, 1)
                    if c4 < NCH - 1:
                        gemm(f"s{c4}")
                gemm("out4")
                pe.wait_ge(oc_ready.sem, oc_ready.at(l))
                for t in range(NT):
                    for b in range(4):
                        e = turn(ps[:, 4 + t, b * P:(b + 1) * P], yc_c[:, t, b * P:(b + 1) * P], ident)
                e.then_inc(oc_turned.sem, 1)

                gemm("bqk")
                turn_tile(T_BQK, tok_a[T_BQK % 2], 6)
                gemm("ret1")
                pe.wait_ge(cat_lo.sem, cat_lo.at(l, 0))
                pe.wait_ge(tile_ch.sem, tile_ch.at(l, TURNED.index(T_BQK)))
                for h in range(R_HEADS):
                    b, o = h // 2, h % 2
                    mm(ps[:, 4 + h, 0:256], bT[rows(o), 2 + b, 0:P], bT[rows(o), b, :], start=True, stop=True)
                    e = mm(ps[:, 4 + h, 256:384], bT[rows(o), 2 + b, P:SEQ], bT[rows(o), b, P:SEQ],
                           start=True, stop=True)
                e.then_inc(bs_ps.sem, 1)
                gemm("ret2")
                pe.wait_ge(sb_ready.sem, sb_ready.at(l))
                pe.wait_ge(tile_tok.sem, tile_tok.at(l, T_BV))
                for h in range(R_HEADS):
                    cols = slice(h * R_V, (h + 1) * R_V)
                    mm(ps[:, 4, cols], SB[:, h, 0:P], bv[:, 0, cols], start=True, stop=True)
                    mm(ps[:, 5, cols], SB[:, h, P:2 * P], bv[:, 0, cols], start=True, stop=False)
                    e = mm(ps[:, 5, cols], SB[:, h, 2 * P:3 * P], bv[:, 1, cols], start=False, stop=True)
                e.then_inc(yb_ps.sem, 1)
                gemm("ret3")
                turn_tile(T_QI0, tok_a[T_QI0 % 2], 6)
                gemm("ret6")
                pe.wait_ge(ob_ready.sem, ob_ready.at(l))
                for t in range(NT):
                    for b in range(4):
                        e = turn(ps[:, 4 + t, b * P:(b + 1) * P], yc_b[:, t, b * P:(b + 1) * P], ident)
                e.then_inc(ob_turned.sem, 1)
                gemm("qi1")
                turn_tile(T_QI1, tok_a[T_QI1 % 2], 6)

                for k in range(8):
                    t = k // 4
                    gemm(f"score{k}")
                    if k == 0:
                        pe.wait_ge(tile_ch.sem, tile_ch.at(l, TURNED.index(T_QI1)))
                        pe.wait_ge(cat_lo.sem, cat_lo.at(l, 1))
                    if k >= 2:
                        pe.wait_ge(relu_ready.sem, relu_ready.at(l, k - 2))
                    for c in range(4):
                        o, pair = c % 2, c // 2
                        e = mm(ps[:, 4 + 2 * (k % 2) + o, 256 * pair:256 * pair + P * (t + 1)],
                               qiT[rows(o), 2 * (k % 4) + pair, t * P:(t + 1) * P],
                               kiT[rows(o), 0:P * (t + 1)], start=True, stop=True)
                    e.then_inc(score_ps.sem, 1)
                gemm("q0")
                pe.wait_ge(relu_ready.sem, relu_ready.at(l, 7))
                turn_tile(T_Q0, tok_a[T_Q0 % 2], 4)
                gemm("k0")
                turn_tile(T_K0, tok_a[T_K0 % 2], 6)

                def products(u):
                    t, h0 = u % 2, 4 * (u // 2)
                    ns = P * (t + 1)
                    for h in range(4):
                        e = mm(flat(banks(4 + 2 * t, 2))[:, h * ns:(h + 1) * ns], qT[:, h0 + h, t * P:(t + 1) * P],
                               kT[:, h0 + h, 0:ns], start=True, stop=True)
                    e.then_inc(att_ps.sem, 1)

                def turn_probs(u):
                    t = u % 2
                    pe.wait_ge(p_ready.sem, p_ready.at(l, u))
                    for h in range(4):
                        for s in range(t + 1):
                            at = ((t + 1) * h + s) * P
                            e = turn(flat(banks(4 + 2 * t, 2))[:, at:at + P], Sx[t][:, h, s * P:(s + 1) * P], ident)
                    e.then_inc(p_turned.sem, 1)

                def attend(u):
                    t = u % 2
                    probs = flat(PT[t][:, :, :, :])
                    pe.wait_ge(pT_ready.sem, pT_ready.at(l, u))
                    for h in range(4):
                        for s in range(t + 1):
                            at = ((t + 1) * h + s) * P
                            e = mm(bank(4 + 2 * t)[:, h * P:(h + 1) * P], v_tok[u // 2][:, s, h * P:(h + 1) * P],
                                   probs[:, at:at + P], start=(s == 0), stop=(s == t))
                    e.then_inc(pv_ps.sem, 1)

                gemm("att0")
                pe.wait_ge(tile_ch.sem, tile_ch.at(l, TURNED.index(T_K0)))
                products(0)
                products(1)
                gemm("pt0")
                turn_probs(0)
                gemm("pt1")
                turn_probs(1)
                gemm("pv0")
                attend(0)
                gemm("pv1")
                attend(1)
                gemm("q1")
                pe.wait_ge(cat_lo.sem, cat_lo.at(l, 2))
                turn_tile(T_Q1, tok_a[T_Q1 % 2], 4)
                gemm("k1")
                pe.wait_ge(cat_lo.sem, cat_lo.at(l, 3))
                turn_tile(T_K1, tok_a[T_K1 % 2], 6)
                gemm("att2")
                pe.wait_ge(tile_ch.sem, tile_ch.at(l, TURNED.index(T_K1)))
                products(2)
                products(3)
                gemm("pt2")
                turn_probs(2)
                gemm("pt3")
                turn_probs(3)
                gemm("pv2")
                attend(2)
                gemm("pv3")
                attend(3)

                gemm("turn0")
                turn_x(2 * l + 1, 0)
                gemm("turn1")
                turn_x(2 * l + 1, 1)
                gemm("turn2")
                turn_x(2 * l + 1, 2)
                gemm("out_end")

                def turn_product(i, g):
                    pe.wait_ge(ffa_ready.sem, g)
                    for t in range(NT):
                        for c in range(4):
                            e = turn(ps[:, 4 + t, c * P:(c + 1) * P], ff_act[:, t, c * P:(c + 1) * P], ident)
                    e.then_inc(ffa_turned.sem, 1)

                def ffn(i, first):
                    n0 = nb + FFN_B0 + i * 8
                    g = i * 1 + (l * FT)
                    if first:
                        x_split(2 * l + 1, 2)
                        pe.wait_ge(resid_out.sem, resid_out.at(l, 2))
                    else:
                        pe.wait_ge(silu_ready.sem, g)
                    for b in range(8):
                        if b == 1 and first:
                            turn_x(2 * l + 1, 3)
                        if b == 3 and first:
                            x_split(2 * l + 1, 3)
                        if b == 2 and not first:
                            turn_product(i, g)
                        mm_block(n0 + (b + 1), b % 2, act_hi, act_lo, KB * (b % 4), KB, TW, 2 * (b // 4),
                                 b % 4 == 0, b % 4 == 3)

                ffn(0, True)
                with pe.Fori(1, FT) as i:
                    ffn(i, False)
                pe.wait_ge(silu_ready.sem, FT * (l + 1))
                pe.wait_ge(ff_lo_ready.sem, FT * (l + 1) - 1)

                for cb in range(4):
                    if cb >= 2:
                        pe.wait_ge(resid_down.sem, resid_down.at(l, cb - 2))
                    for b in range(DOWN_PER):
                        if b == 3 and cb > 0 and l < DEPTH - 1:
                            turn_x(2 * l + 2, cb - 1)
                        if b == 1 and cb == 0:
                            turn_product(FT - 1, FT * (l + 1))
                        if b == DOWN_PER - 1 and cb == 0:
                            pe.wait_ge(ff_lo_ready.sem, FT * (l + 1))
                        n = nb + DOWN_B0 + DOWN_PER * cb + b
                        mm_block(n + 1, n % 2, ff_hi, ff_lo, KB * b, KB, TW, 2 * (cb % 2), b == 0, b == DOWN_PER - 1)


def _constants():
    pos = np.arange(SEQ, dtype=np.float32)
    tabs = []
    for half, theta in ((A_HALF, 500000.0), (I_HALF, 500000.0), (R_HALF, 10000.0)):
        freqs = np.power(np.float32(theta), -np.arange(half, dtype=np.float32) / np.float32(half))
        ang = pos[:, None] * freqs[None, :].astype(np.float32)
        tabs += [np.cos(ang), np.sin(ang)]
    rope = np.concatenate(tabs, axis=1).reshape(NT, P, -1).transpose(1, 0, 2).reshape(P, -1)
    p = np.arange(P)
    headmask = np.zeros((P, 4, 8), np.float32)
    for b in range(4):
        headmask[p, b, 2 * b + p // W_DIM] = 1
    s, t = p[:, None] % CH, np.arange(CH)[None, :]
    strict, inclusive = s < t, s <= t
    gram = np.concatenate([strict, inclusive, strict, inclusive], axis=1)
    level = [(s >> (k + 1) == t >> (k + 1)) & (s >> k & 1 == 0) & (t >> k & 1 == 1) for k in range(6)]
    consts = np.concatenate([np.eye(P), rope, headmask.reshape(P, -1), gram, *level, s == t],
                            axis=1).astype(np.float32)
    assert consts.shape == (P, N_CONST)
    log_g = np.log1p(-np.power(2.0, -5.0 - np.arange(R_HEADS)))
    m, n = p[:, None], np.arange(SEQ)[None, :]
    whole = np.where(n >= m, 1.0, 0.0) * np.exp(np.maximum(n - m, 0)[None] * log_g[:, None, None])
    decay = np.concatenate([whole, whole[:, :, 0:P]], axis=2).transpose(1, 0, 2) * R_QK ** -0.5
    headmask_t = headmask.transpose(2, 1, 0).reshape(8, 4 * P)
    return consts, decay.reshape(P, -1).astype(np.float32), np.ascontiguousarray(headmask_t)


def _blocks(w, kb=KB):
    k, n = w.shape
    return w.reshape(k // (kb * P), kb, P, n).transpose(0, 2, 1, 3).reshape(-1, P, kb * n)


def _stream(w_in, w_in_vres, w_out, w_gate_up, w_down):
    s = np.zeros((N_BLOCKS, P, BLK), w_in.dtype)
    full = [(T_R, C0), (T_K, C0 + C_W), (T_V, C0 + 2 * C_W), (T_QI0, QI0), (T_QI1, QI0 + TW), (T_Q0, Q0),
            (T_Q1, Q0 + TW), (T_K0, K0), (T_K1, K0 + TW), (T_V0, V0), (T_V1, V0 + TW), (T_BQK, BQ0),
            (T_BV, BV0), (T_BG, BG0)]
    for l in range(DEPTH):
        nb = l * LAYER_BLOCKS
        for j, c in full:
            s[nb + first_block(j):nb + first_block(j + 1)] = _blocks(w_in[l][:, c:c + TW])
        tail = np.zeros((D, TW), w_in.dtype)
        tail[:, 0:DECAY_LORA] = w_in[l][:, WL0:AL0]
        tail[:, P:P + AAA_LORA] = w_in[l][:, AL0:GL0]
        tail[:, 2 * P:] = w_in[l][:, GL0:GL0 + GATE_LORA]
        if l > 0:
            for k in range(2):
                half = w_in_vres[l - 1][:, k * MV_LORA // 2:(k + 1) * MV_LORA // 2]
                tail[:, (k + 1) * P - MV_LORA // 2:(k + 1) * P] = half
        s[nb + first_block(T_TAIL):nb + first_block(T_NARROW)] = _blocks(tail)
        narrow = w_in[l][:, KI0:BQ0]
        s[nb + first_block(T_NARROW):nb + first_block(T_V0), :, 0:NARROW_KB * NARROW] = _blocks(narrow, NARROW_KB)
        for c in range(4):
            cols = slice(c * TW, (c + 1) * TW)
            rows = _blocks(w_out[l][:, cols])
            for at, (cb, q) in enumerate(OUT_ORDER):
                if cb == c:
                    s[nb + OUT_B0 + at] = rows[q]
            s[nb + DOWN_B0 + DOWN_PER * c:nb + DOWN_B0 + DOWN_PER * (c + 1)] = _blocks(w_down[l][:, cols])
        for f in range(FT):
            for part in range(2):
                at = nb + FFN_B0 + 8 * f + 4 * part
                c = part * D_FF + f * TW
                s[at:at + 4] = _blocks(w_gate_up[l][:, c:c + TW])
    return s.reshape(N_BLOCKS * P, BLK)


def _vectors(i):
    v = np.zeros((P, DEPTH, N_VEC), np.float32)

    def put(l, name, a, rows=P):
        at, n = VEC[name]
        v[0:rows, l, at:at + n] = np.asarray(a).reshape(n, rows).T

    for l in range(DEPTH):
        mu = i["rwkv_mu"][l]
        o = 3 * C_W
        put(l, "mu_r", mu[0:C_W])
        put(l, "mu_k", mu[C_W:2 * C_W])
        put(l, "mu_v", mu[2 * C_W:o])
        put(l, "mu_wl", mu[o:o + DECAY_LORA], DECAY_LORA)
        put(l, "mu_al", mu[o + DECAY_LORA:o + DECAY_LORA + AAA_LORA], AAA_LORA)
        put(l, "mu_gl", mu[o + DECAY_LORA + AAA_LORA:])
        put(l, "w0", i["rwkv_w0"][l])
        put(l, "a0", i["rwkv_a0"][l])
        put(l, "k_k", i["rwkv_k_k"][l])
        put(l, "k_a", i["rwkv_k_a"][l])
        put(l, "r_k", i["rwkv_r_k"][l])
        if l > 0:
            for k, name in enumerate(("mu_wl", "mu_al")):
                v[P - MV_LORA // 2:, l, VEC[name][0]] = \
                    i["rwkv_mu_vres"][l - 1][k * MV_LORA // 2:(k + 1) * MV_LORA // 2]
            put(l, "v0", i["rwkv_v0"][l - 1])
    return v.reshape(P, DEPTH * N_VEC)


def kernel(**inputs):
    import concourse.bacc as _bacc
    from concourse.bass_utils import run_bass_kernel_spmd as _run

    i = {k: np.asarray(v) for k, v in inputs.items()}
    consts, decay, headmask_t = _constants()
    gain_cols = np.concatenate([g.reshape(KT, P).T for l in range(DEPTH)
                                for g in (i["norm_mix_g"][l], i["norm_ffn_g"][l])], axis=1)
    vlb = np.zeros((2, P, C_W), np.float32)
    vlb[:, P - MV_LORA // 2:] = i["rwkv_v_lora_b"][0].reshape(2, MV_LORA // 2, C_W)
    vlb = vlb.reshape(2 * P, C_W)
    arrays = {
        "x_in": i["x"].reshape(SEQ, D),
        "stream": _stream(i["w_in"], i["w_in_vres"], i["w_out"], i["w_gate_up"], i["w_down"]),
        "consts": consts, "decay_in": decay, "headmask_t": headmask_t, "vecs": _vectors(i),
        "wlb": i["rwkv_w_lora_b"], "alb": i["rwkv_a_lora_b"], "vlb": vlb,
        "glb": i["rwkv_g_lora_b"],
        "lnx": np.concatenate([i["rwkv_lnx_g"], i["rwkv_lnx_b"]], axis=1),
        "gain_cols": gain_cols, "final_gain": i["final_norm_g"].reshape(1, D),
    }
    nc = _bacc.Bacc("TRN2", target_bir_lowering=False, num_devices=1, dynamic_dma_scratch_size=8192)
    args, maps = {}, {}
    for name, a in arrays.items():
        a = np.ascontiguousarray(a)
        maps[name + "_dram"] = a
        args[name] = nc.dram_tensor(name + "_dram", a.shape, mybir.dt.from_np(a.dtype), kind="ExternalInput").ap()
    v_keep = nc.dram_tensor("v_keep_dram", (P, 4 * SEQ), F32, kind="Internal").ap()
    x_keep = nc.dram_tensor("x_keep_dram", (SEQ, D), F32, kind="Internal").ap()
    out = nc.dram_tensor("out_dram", (SEQ, D), F32, kind="ExternalOutput").ap()
    build(nc, out=out, v_keep=v_keep, x_keep=x_keep, **args)
    r = _run(nc, [maps], core_ids=[0])
    return r.results[0]["out_dram"].reshape(1, SEQ, D)
```
